# Optimizing a Trainium2 kernel written in Bass

```python
import math
import jax, jax.numpy as jnp
from jax import lax
import numpy as np

D_MODEL = 1024
BATCH = 1
SEQ = 512
DEPTH = 2
DEC_BATCH = 8
DEC_SEQ = 4
PAST_LEN = 1024
PAGE_SIZE = 128

N_ATTN_LAYERS = (DEPTH + 1) // 2
N_CONV_LAYERS = DEPTH // 2
A_WIDTH = D_MODEL // 2
HD_A = 64
H_A = A_WIDTH // (2 * HD_A)
DK_A = 2 * HD_A
DV_A = 2 * HD_A
B_WIDTH = D_MODEL - A_WIDTH
CONV_B_WIDTH = 31
C_WIDTH = D_MODEL
CONV_C_WIDTH = 3
IN_EVEN = 3 * A_WIDTH + 2 * B_WIDTH
N_GROUPS = 4
EXPERTS_PER_GROUP = 8
N_EXPERTS = N_GROUPS * EXPERTS_PER_GROUP
TOP_K_IN_GROUP = 2
F_EXPERT = 512
MOE_BLOCK = 128
Q_BLOCK = 128
ALIBI_MAX = 8.0
EPS = 1e-6
NEG_BIG = -1e30

kernel_name = 'hybrid_diffattn_conformer_shortconv_hmoe_step'

def rmsnorm(x, g):
    x32 = x.astype(jnp.float32)
    y = x32 * lax.rsqrt(jnp.mean(x32 * x32, axis=-1, keepdims=True) + EPS)
    return (y * g.astype(jnp.float32)).astype(x.dtype)

def layernorm(x, g, b):
    x32 = x.astype(jnp.float32)
    mu = jnp.mean(x32, axis=-1, keepdims=True)
    xc = x32 - mu
    y = xc * lax.rsqrt(jnp.mean(xc * xc, axis=-1, keepdims=True) + EPS)
    return (y * g.astype(jnp.float32) + b.astype(jnp.float32)).astype(x.dtype)

def causal_dwconv(u, buf, w):
    xp = jnp.concatenate([buf.astype(u.dtype), u], axis=1)
    y = lax.conv_general_dilated(xp, w.astype(u.dtype), window_strides=(1,), padding='VALID',
                                 dimension_numbers=('NWC', 'WIO', 'NWC'), feature_group_count=u.shape[-1])
    new_buf = xp[:, xp.shape[1] - (w.shape[0] - 1):]
    return y, new_buf

def ada_mod(c, w, b):
    return jnp.split(jax.nn.silu(c) @ w + b, 6, axis=-1)

def modulate(x, g, shift, scale):
    return rmsnorm(x, g) * (1 + scale[:, None, :]) + shift[:, None, :]

def diff_attn_core(q, k, v, q_pos, k_pos, lam):
    slopes = jnp.exp2(-ALIBI_MAX * jnp.arange(1, H_A + 1, dtype=jnp.float32) / H_A)
    dist = (q_pos[:, None] - k_pos[None, :]).astype(jnp.float32)
    bias = -slopes[:, None, None] * jnp.abs(dist)
    causal = dist >= 0
    scale = HD_A ** -0.5

    def attn_map(qa, ka):
        s = jnp.einsum('bqhd,bkhd->bhqk', qa, ka).astype(jnp.float32) * scale + bias
        return jax.nn.softmax(jnp.where(causal, s, NEG_BIG), axis=-1)

    p = attn_map(q[..., :HD_A], k[..., :HD_A]) - lam * attn_map(q[..., HD_A:], k[..., HD_A:])
    return jnp.einsum('bhqk,bkhd->bqhd', p.astype(v.dtype), v)

def even_mixer(h, k_past, v_past, conv_buf, w_in, q_gain, k_gain, lam_q1, lam_k1, lam_q2, lam_k2,
               lam_init, sub_gain, cb_w, cb_b, cb_ln_g, cb_ln_b, w_out):
    bn, t, _ = h.shape
    proj = h @ w_in
    q, k, v, ga, gb = jnp.split(proj, [A_WIDTH, 2 * A_WIDTH, 3 * A_WIDTH, 3 * A_WIDTH + B_WIDTH], axis=-1)
    q = rmsnorm(q.reshape(bn, t, H_A, 2, HD_A), q_gain).reshape(bn, t, H_A, DK_A)
    k = rmsnorm(k.reshape(bn, t, H_A, 2, HD_A), k_gain).reshape(bn, t, H_A, DK_A)
    v = v.reshape(bn, t, H_A, DV_A)
    lam = (jnp.exp(jnp.sum((lam_q1 * lam_k1).astype(jnp.float32)))
           - jnp.exp(jnp.sum((lam_q2 * lam_k2).astype(jnp.float32))) + lam_init)
    if k_past is None:
        pos = jnp.arange(t, dtype=jnp.int32)
        nb = t // Q_BLOCK
        qb = jnp.moveaxis(q.reshape(bn, nb, Q_BLOCK, H_A, DK_A), 1, 0)
        pb = pos.reshape(nb, Q_BLOCK)
        ob = lax.map(lambda a: diff_attn_core(a[0], k, v, a[1], pos, lam), (qb, pb))
        o = jnp.moveaxis(ob, 0, 1).reshape(bn, t, H_A, DV_A)
    else:
        past = k_past.shape[1]
        k_all = jnp.concatenate([k_past.astype(k.dtype), k], axis=1)
        v_all = jnp.concatenate([v_past.astype(v.dtype), v], axis=1)
        k_pos = jnp.arange(past + t, dtype=jnp.int32)
        q_pos = past + jnp.arange(t, dtype=jnp.int32)
        o = diff_attn_core(q, k_all, v_all, q_pos, k_pos, lam)
    o = (rmsnorm(o, sub_gain) * (1.0 - lam_init)).reshape(bn, t, A_WIDTH)
    u = ga * jax.nn.sigmoid(gb)
    cv, new_buf = causal_dwconv(u, conv_buf, cb_w)
    cv = jax.nn.silu(layernorm(cv + cb_b, cb_ln_g, cb_ln_b))
    out = jnp.concatenate([o, cv], axis=-1) @ w_out
    return out, k, v, new_buf

def odd_mixer(h, conv_buf, w_in, conv_w, w_out):
    bg, cg, hx = jnp.split(h @ w_in, 3, axis=-1)
    y, new_buf = causal_dwconv(cg * hx, conv_buf, conv_w)
    return (bg * y) @ w_out, new_buf

def hier_moe(x, w_group, b_group, w_router, b_router, w_gate_up, w_down):
    bn, t, d = x.shape
    xf = x.reshape(-1, d)
    n = xf.shape[0]
    g_logits = (xf @ w_group).astype(jnp.float32) + b_group
    g_idx = jnp.argmax(g_logits, axis=-1)
    g_w = jnp.take_along_axis(jax.nn.softmax(g_logits, axis=-1), g_idx[:, None], axis=-1)
    e_logits = ((xf @ w_router).astype(jnp.float32) + b_router).reshape(n, N_GROUPS, EXPERTS_PER_GROUP)
    e_in_group = jnp.take_along_axis(e_logits, g_idx[:, None, None], axis=1)[:, 0]
    top_v, top_i = lax.top_k(e_in_group, TOP_K_IN_GROUP)
    weights = g_w * jax.nn.softmax(top_v, axis=-1)
    expert = (g_idx[:, None] * EXPERTS_PER_GROUP + top_i).reshape(-1).astype(jnp.int32)
    nk = n * TOP_K_IN_GROUP
    order = jnp.argsort(expert)
    e_sorted = expert[order]
    tok_sorted = order // TOP_K_IN_GROUP
    w_sorted = weights.reshape(-1)[order]
    sizes = jnp.bincount(expert, length=N_EXPERTS).astype(jnp.int32)
    padded = ((sizes + MOE_BLOCK - 1) // MOE_BLOCK) * MOE_BLOCK
    pad_end = jnp.cumsum(padded)
    pad_start = pad_end - padded
    start = jnp.cumsum(sizes) - sizes
    dest = pad_start[e_sorted] + jnp.arange(nk, dtype=jnp.int32) - start[e_sorted]
    n_blocks = (nk + MOE_BLOCK - 1) // MOE_BLOCK + N_EXPERTS
    xp = jnp.zeros((n_blocks * MOE_BLOCK, d), x.dtype).at[dest].set(xf[tok_sorted])
    block_e = jnp.minimum(jnp.searchsorted(pad_end, jnp.arange(n_blocks, dtype=jnp.int32) * MOE_BLOCK, side='right'),
                          N_EXPERTS - 1)

    def expert_block(a):
        xb, e = a
        gate, up = jnp.split(xb @ w_gate_up[e], 2, axis=-1)
        return (jax.nn.silu(gate) * up) @ w_down[e]

    yp = lax.map(expert_block, (xp.reshape(n_blocks, MOE_BLOCK, d), block_e)).reshape(-1, d)
    y = jax.ops.segment_sum(yp[dest] * w_sorted[:, None].astype(x.dtype), tok_sorted, num_segments=n)
    return y.reshape(bn, t, d)

def setup_inputs(seed: int = 0) -> dict:
    key = jax.random.key(seed)
    ks = iter(jax.random.split(key, 40))
    f32 = jnp.float32

    def nrm(shape, scale):
        return jax.random.normal(next(ks), shape, f32) * scale

    def gain(shape):
        return 1.0 + nrm(shape, 0.05)

    n_pages = PAST_LEN // PAGE_SIZE
    n_pool = (DEC_BATCH * n_pages * 5) // 4
    d = D_MODEL
    inp = {}
    inp['x_prompt'] = nrm((BATCH, SEQ, d), 1.0)
    inp['x_sample'] = nrm((DEC_BATCH, DEC_SEQ, d), 1.0)
    inp['cache_k'] = nrm((N_ATTN_LAYERS, n_pool, PAGE_SIZE, H_A, DK_A), 1.0)
    inp['cache_v'] = nrm((N_ATTN_LAYERS, n_pool, PAGE_SIZE, H_A, DV_A), 1.0)
    inp['state_conv_b'] = nrm((N_ATTN_LAYERS, DEC_BATCH, CONV_B_WIDTH - 1, B_WIDTH), 0.5)
    inp['state_conv_c'] = nrm((N_CONV_LAYERS, DEC_BATCH, CONV_C_WIDTH - 1, C_WIDTH), 0.5)
    inp['page_table'] = jax.random.permutation(next(ks), n_pool)[: DEC_BATCH * n_pages].reshape(
        DEC_BATCH, n_pages).astype(jnp.int32)
    inp['c_prompt'] = nrm((BATCH, d), 1.0)
    inp['c_sample'] = nrm((DEC_BATCH, d), 1.0)
    inp['norm_mix_g'] = gain((DEPTH, d))
    inp['norm_ffn_g'] = gain((DEPTH, d))
    inp['w_ada'] = nrm((DEPTH, d, 6 * d), 0.02)
    inp['b_ada'] = nrm((DEPTH, 6 * d), 0.01)
    inp['w_in_a'] = nrm((N_ATTN_LAYERS, d, IN_EVEN), d ** -0.5)
    inp['q_norm_g'] = gain((N_ATTN_LAYERS, 2, HD_A))
    inp['k_norm_g'] = gain((N_ATTN_LAYERS, 2, HD_A))
    inp['lam_q1'] = nrm((N_ATTN_LAYERS, HD_A), 0.1)
    inp['lam_k1'] = nrm((N_ATTN_LAYERS, HD_A), 0.1)
    inp['lam_q2'] = nrm((N_ATTN_LAYERS, HD_A), 0.1)
    inp['lam_k2'] = nrm((N_ATTN_LAYERS, HD_A), 0.1)
    inp['subln_g'] = gain((N_ATTN_LAYERS, DV_A))
    inp['convb_w'] = nrm((N_ATTN_LAYERS, CONV_B_WIDTH, 1, B_WIDTH), CONV_B_WIDTH ** -0.5)
    inp['convb_b'] = nrm((N_ATTN_LAYERS, B_WIDTH), 0.01)
    inp['convb_ln_g'] = gain((N_ATTN_LAYERS, B_WIDTH))
    inp['convb_ln_b'] = nrm((N_ATTN_LAYERS, B_WIDTH), 0.01)
    inp['w_out_a'] = nrm((N_ATTN_LAYERS, A_WIDTH + B_WIDTH, d), (A_WIDTH + B_WIDTH) ** -0.5)
    inp['w_in_c'] = nrm((N_CONV_LAYERS, d, 3 * C_WIDTH), d ** -0.5)
    inp['convc_w'] = nrm((N_CONV_LAYERS, CONV_C_WIDTH, 1, C_WIDTH), CONV_C_WIDTH ** -0.5)
    inp['w_out_c'] = nrm((N_CONV_LAYERS, C_WIDTH, d), C_WIDTH ** -0.5)
    inp['w_group'] = nrm((DEPTH, d, N_GROUPS), d ** -0.5)
    inp['b_group'] = nrm((DEPTH, N_GROUPS), 0.01)
    inp['w_router'] = nrm((DEPTH, d, N_EXPERTS), d ** -0.5)
    inp['b_router'] = nrm((DEPTH, N_EXPERTS), 0.01)
    inp['w_gate_up'] = nrm((DEPTH, N_EXPERTS, d, 2 * F_EXPERT), d ** -0.5)
    inp['w_down'] = nrm((DEPTH, N_EXPERTS, F_EXPERT, d), F_EXPERT ** -0.5)
    return inp

def reference(x_prompt, x_sample, cache_k, cache_v, state_conv_b, state_conv_c, page_table, c_prompt, c_sample,
              norm_mix_g, norm_ffn_g, w_ada, b_ada, w_in_a, q_norm_g, k_norm_g, lam_q1, lam_k1, lam_q2, lam_k2,
              subln_g, convb_w, convb_b, convb_ln_g, convb_ln_b, w_out_a, w_in_c, convc_w, w_out_c,
              w_group, b_group, w_router, b_router, w_gate_up, w_down):
    xp, xs = x_prompt, x_sample
    bp, bs = xp.shape[0], xs.shape[0]
    k_p, v_p, k_s, v_s, cb_p, cb_s, cc_p, cc_s = [], [], [], [], [], [], [], []
    for l in range(DEPTH):
        sh1p, sc1p, g1p, sh2p, sc2p, g2p = ada_mod(c_prompt, w_ada[l], b_ada[l])
        sh1s, sc1s, g1s, sh2s, sc2s, g2s = ada_mod(c_sample, w_ada[l], b_ada[l])
        hp = modulate(xp, norm_mix_g[l], sh1p, sc1p)
        hs = modulate(xs, norm_mix_g[l], sh1s, sc1s)
        i = l // 2
        if l % 2 == 0:
            lam_init = 0.8 - 0.6 * math.exp(-0.3 * l)
            prm = (w_in_a[i], q_norm_g[i], k_norm_g[i], lam_q1[i], lam_k1[i], lam_q2[i], lam_k2[i], lam_init,
                   subln_g[i], convb_w[i], convb_b[i], convb_ln_g[i], convb_ln_b[i], w_out_a[i])
            zero_buf = jnp.zeros((bp, CONV_B_WIDTH - 1, B_WIDTH), xp.dtype)
            op, kp_new, vp_new, bufp = even_mixer(hp, None, None, zero_buf, *prm)
            k_past = cache_k[i][page_table].reshape(bs, -1, H_A, DK_A)
            v_past = cache_v[i][page_table].reshape(bs, -1, H_A, DV_A)
            os_, ks_new, vs_new, bufs = even_mixer(hs, k_past, v_past, state_conv_b[i], *prm)
            k_p.append(kp_new)
            v_p.append(vp_new)
            k_s.append(ks_new)
            v_s.append(vs_new)
            cb_p.append(bufp)
            cb_s.append(bufs)
        else:
            zero_buf = jnp.zeros((bp, CONV_C_WIDTH - 1, C_WIDTH), xp.dtype)
            op, bufp = odd_mixer(hp, zero_buf, w_in_c[i], convc_w[i], w_out_c[i])
            os_, bufs = odd_mixer(hs, state_conv_c[i], w_in_c[i], convc_w[i], w_out_c[i])
            cc_p.append(bufp)
            cc_s.append(bufs)
        xp = xp + g1p[:, None, :] * op
        xs = xs + g1s[:, None, :] * os_
        hp = modulate(xp, norm_ffn_g[l], sh2p, sc2p)
        hs = modulate(xs, norm_ffn_g[l], sh2s, sc2s)
        moe_prm = (w_group[l], b_group[l], w_router[l], b_router[l], w_gate_up[l], w_down[l])
        xp = xp + g2p[:, None, :] * hier_moe(hp, *moe_prm)
        xs = xs + g2s[:, None, :] * hier_moe(hs, *moe_prm)
    return (xp, xs, jnp.stack(k_p), jnp.stack(v_p), jnp.stack(k_s), jnp.stack(v_s),
            jnp.stack(cb_p), jnp.stack(cb_s), jnp.stack(cc_p), jnp.stack(cc_s))


_drawn_inputs = setup_inputs


def setup_inputs(seed=0):
    import zlib

    import numpy as np

    out = dict(_drawn_inputs(seed))
    spreads = {}
    factors = {'q_norm_g': 3.147,
     'subln_g': 2.814,
     'convb_b': 8.0,
     'convb_ln_b': 25.515,
     'b_group': 24.671,
     'b_router': 14.873,
     'convb_ln_g': 3.912}
    for name, (base, spread) in spreads.items():
        noise = np.random.default_rng([zlib.crc32(name.encode()), seed]).standard_normal(out[name].shape)
        drawn = base * np.exp(spread * noise) if base else spread * noise
        out[name] = __import__('jax').numpy.asarray(drawn.astype(out[name].dtype))
    for name, factor in factors.items():
        out[name] = (out[name] * factor).astype(out[name].dtype)
    return out
```

```python
from contextlib import ExitStack

import numpy as np

import concourse.bass as bass
from concourse import mybir

F32 = mybir.dt.float32
I32 = mybir.dt.int32
ALU = mybir.AluOpType
ACT = mybir.ActivationFunctionType
AX = mybir.AxisListType.X

P = 128
D = 1024
KD = D // P
TP, NSEQ, TS = 512, 8, 4
NS = NSEQ * TS
T = TP + NS
NT = TP // P + 1
LS = NT - 1
H, HD = 4, 64
PAST, PAGE = 1024, 128
NPG = PAST // PAGE
BW = 31
PAD = BW - 1
E, G, EG = 32, 4, 8
FE = 512
CAP = 64
NB = -(-T // CAP)
PAIRS = E // 2
OOB = 6000.0
BIG = 1e30
EPS = 1e-6
LAM_INIT = 0.2
NR = E + G
MODS = 6
SLOT = 4096
NSLOT = 6

C_ID, C_ONE, C_UP, C_I32, C_I32M, C_GRPM, C_VALID, C_A1, C_T, C_EPS, C_SEL, NC = (
    np.cumsum([0, P, P, P, E, E, E, NT, 2 * NT, NT, 1, 2 * 4 * H]).tolist())


def constants():
    c = np.zeros((P, NC), np.float32)
    p = np.arange(P)
    c[:, C_ID:C_ID + P] = np.eye(P)
    c[:, C_ONE:C_ONE + P] = 1
    c[:, C_UP:C_UP + P] = p[:, None] < p[None, :]
    c[:, C_I32:C_I32 + E] = np.arange(E)
    c[:, C_I32M:C_I32M + E] = np.arange(E) - 99
    c[:, C_GRPM:C_GRPM + E] = np.arange(E) // EG - 99
    tok = p[:, None] + P * np.arange(NT)
    c[:, C_VALID:C_VALID + NT] = tok < T
    c[:, C_A1:C_A1 + 2 * NT] = (2 * tok[:, :, None] + np.arange(2) + 1).reshape(P, -1)
    c[:, C_T:C_T + NT] = tok
    c[:, C_EPS] = EPS
    r = np.arange(8 * H)
    for m in range(2):
        c[r, C_SEL + 16 * m + 4 * (r // 8) + r % 4] = (r // 4 % 2) == m
    return c


def slot_numbers():
    return np.tile(np.arange(NB * CAP, dtype=np.float32), (P, 1))


def prompt_bias():
    p, j = np.arange(P)[:, None], np.arange(TP)[None, :]
    dist = p - j + (TP - P)
    return np.stack([np.where(dist >= 0, -2.0 ** (-2 * (h + 1)) * dist, -BIG) for h in range(H)], 1).reshape(
        P, H * TP).astype(np.float32)


def sample_bias():
    r = np.arange(8 * H)
    slope, t = -2.0 ** (-2.0 * (r // 8 + 1)), r % 4
    past = slope[:, None] * (PAST + t[:, None] - np.arange(PAST)[None, :])
    key = np.arange(NS)
    new = []
    for b in range(NSEQ):
        dist = t[:, None] - (key % TS)[None, :]
        new.append(np.where((key[None, :] // TS == b) & (dist >= 0), slope[:, None] * dist, -BIG))
    return np.concatenate([past] + new, 1).astype(np.float32)


W_PRM, W_C, W_LAM = 0, 512, 1536
W_U, W_US, W_CV, W_V, W_RAW, W_SG = 0, 2168, 3256, 5432, 7992, 9528
W_N = W_SG + T
W_PT, W_E = W_RAW, W_CV
W_QB, W_S, W_PS, W_KT, W_QC, W_QN = 2168, 3256, 4312, 7992, 9016, 9144
W_SQ, W_RN = W_CV, W_V
W_VP, W_CG, W_Y3, W_VS, W_VK, W_VN, W_ST, W_SO = 0, 514, 1602, 2146, 2530, 2546, 3072, 4096
W_AP, W_BP, W_AS, W_BS = 0, 1024, 2048, 3072
R_LG, R_ME, R_A1, R_A2, R_CC, R_T, R_M2 = 4096, 4280, 4440, 4600, 4760, 4920, 5080
W_OH, W_V3, W_LI, W_LW, W_SLOT = 5300, 6452, 8312, 8888, 9176
W_XG, W_XT, W_GT, W_HH, W_Y = 0, 2048, 3072, 3584, 4096
W_YB, W_G, W_GS = 2048, 6200, 7224
W_RA, W_RB = 9760, 5300
W_SLOT_END = W_SLOT + NB * CAP
assert W_SLOT_END <= W_RA and W_RA + KD * NS <= W_N and W_V3 + 960 <= W_LI


def hybrid_step(nc, a, o):
    with ExitStack() as ctx:
        def sb(name, shape, dt=F32):
            return ctx.enter_context(nc.sbuf_tensor(name, shape, dt))

        def sem(name):
            return ctx.enter_context(nc.semaphore(name))

        ring = sb("ring", [P, NSLOT, SLOT])
        X = sb("X", [P, NT, D])
        Hb = sb("Hb", [P, NT, D])
        hT = sb("hT", [P, KD, T])
        W = sb("W", [P, W_N])
        C = sb("C", [P, NC])
        modT = sb("modT", [P, 2 * MODS * KD, 9])
        scT = sb("scT", [P, 4, KD, 9])
        wr = sb("wr", [P, 2, KD, NR])
        rb = sb("rb", [P, 2, NR])
        prm = sb("prm", [P, 289])
        qkg = sb("qkg", [P, 2, P])
        lamw = sb("lamw", [P, 8])
        cT = sb("cT", [P, KD, 9])
        st = sb("st", [P, 96])
        cmb = sb("cmb", [8 * H, 32])
        pgt = sb("pgt", [1, NSEQ * NPG], I32)
        tabf = sb("tabf", [1, PAIRS + 1, 4])
        tab = [sb(f"tab{l}", [1, PAIRS + 1, 4], I32) for l in range(2)]
        ix = [sb(f"ix{j}", [CAP, 2], I32) for j in range(2)]
        wj = [sb(f"wj{j}", [CAP, 1]) for j in range(2)]
        ps = ctx.enter_context(nc.psum_tensor("ps", [P, 8, 512], F32))
        h_dram = nc.dram_tensor("h_rows", (T, D), F32).ap()
        y_dram = nc.dram_tensor("y_rows", (2 * T, D), F32).ap()

        ident, ones, upper = C[:, C_ID:C_ID + P], C[:, C_ONE:C_ONE + P], C[:, C_UP:C_UP + P]
        epsc = C[:, C_EPS:C_EPS + 1]
        bT = prm[:, 0:96]
        gT = prm[:, 96:128].rearrange("p (n c) -> p n c", c=KD)
        cbb, lng, lnb, subg = prm[:, 128:132], prm[:, 132:136], prm[:, 136:140], prm[:, 140:141]
        ccw = prm[:, 141:165].rearrange("p (w c) -> p w c", c=KD)
        cbw = prm[:, 165:289].rearrange("p (w c) -> p w c", c=4)
        neglam = lamw[:, 4:5]

        def w(at, *dims, rows=P):
            v = W[0:rows, at:at + int(np.prod(dims))]
            if len(dims) == 1:
                return v
            n = "abcd"[:len(dims)]
            return v.rearrange(f"p ({' '.join(n)}) -> p {' '.join(n)}", **dict(zip(n, dims)))

        def bank(b, *dims, rows=P, at=0):
            v = ps[0:rows, b, at:at + int(np.prod(dims))]
            if len(dims) == 1:
                return v
            n = "abcd"[:len(dims)]
            return v.rearrange(f"p ({' '.join(n)}) -> p {' '.join(n)}", **dict(zip(n, dims)))

        uT, uS = w(W_U, 4, PAD + TP), w(W_US, 4, NSEQ, PAD + TS)
        cv, V, raw, sg = w(W_CV, 4, T), w(W_V, NT, 512), w(W_RAW, 3, 512), w(W_SG, T)
        hflat = Hb[:, :, :].rearrange("p a b -> p (a b)")
        QT = hflat[:, 0:H * T].rearrange("p (h t) -> p h t", h=H)
        KT = hflat[:, H * T:2 * H * T].rearrange("p (h t) -> p h t", h=H)
        sq = hflat[:, 2 * H * T:2 * H * T + 512]
        zT = hflat[:, 0:KD * T].rearrange("p (c t) -> p c t", c=KD)
        vS, vK, vN = w(W_VS, KD, NSEQ, 2 + TS), w(W_VK, KD, 2), w(W_VN, KD, NS)

        def rows(i):
            return P if i < LS else NS

        def toks(i):
            return slice(P * i, P * i + rows(i))

        def mod(l, m):
            return modT[:, MODS * KD * l + KD * m:MODS * KD * l + KD * m + KD, :]

        slot_in = [sem(f"slot_in{s}") for s in range(NSLOT)]
        slot_free = [sem(f"slot_free{s}") for s in range(NSLOT)]
        phase_end = sem("phase_end")
        S = {n: sem(n) for n in (
            "params_in x_in page_in stats_set c_silu c_tr c_ev prm_tr prm_ev lam_sum lam_exp ada_ev "
            "u_mm u_sig u_ok u_state st_tr st_ev conv un_ok uo_tr uo_ev "
            "tok_mm tok_copy tok_sq tok_ss tok_root tok_n tok_g tok_tr tok_ev kv_out "
            "bias_in at_s at_b at_m at_e at_p at_tr at_pt at_o at_ov "
            "qb_ok sp_q sp_kt sp_eva sp_evd sp_s sp_d sp_e sp_pt sp_ptev sp_ov "
            "on_sq on_mm on_root on_ok ln_mm ln_x ln_sq ln_root ln_n out_dma "
            "bch_mm cg_ok z_ok vs_in vs_tr vs_ok vo_tr vo_ok dve carried").split()}
        per_layer = dict(rms1_sum=NT, rms1_root=1, rms1_inv=1, rms2_sum=NT, rms2_root=1, xn_a=2, xn_d=3, tr1=KD + 1,
                         ev1a=4, ev1d=5, gate_mm=1, gate_ev=4, wo_mm=2 * NT, wo_mul=2 * NT, wo_add=2 * NT, bc_mm=1,
                         bc_ev=8, rep_ok=4, h_mul=NT, h_ok=NT, h_out=16 * NT, slots_in=16, tr2=KD + 1, ev2a=4, ev2d=5, lg_mm=1,
                         r_dif=1, r_exp=1, r_ok=1, cnt_mm=1, oh_ok=2 * NT, list_mm=2 * NT, bounds=1, gate2_mm=1,
                         gate2_ev=4, y_in0=48, y_in1=32, y_mul=NT, y_add=NT)
        L = {n: sem(n) for n in per_layer}

        def layer_wait(eng, l, name, n):
            eng.wait_ge(L[name], per_layer[name] * l + n)

        M = [{n: sem(f"{n}_{j}") for n in
              "idx gathered xt_mm xt_ok gu_mm silu_ok h_ok down_mm ya_ok yd_ok scattered".split()}
             for j in range(2)]

        seq = 16 * NPG
        in0 = [80 + 4 * seq] * 4 + [96, 80]
        in1 = [in0[s] + 16 * PAIRS + (32 if s < 2 else 16) for s in range(NSLOT)]
        base_in = [in0, in1]

        def linker(eng, name):
            n = [0]

            def link(ins):
                n[0] += 1
                ins.then_inc(S[name], 1)
                eng.wait_ge(S[name], n[0])
            return link

        def meet(eng, k):
            eng.drain().then_inc(phase_end, 1)
            eng.wait_ge(phase_end, 4 * (k + 1))

        def passes(eng, l, i):
            return [eng.value_load(tab[l][0:1, bass.ds(i, 1), q:q + 1], min_val=q % 2, max_val=2 * E * NB)
                    for q in range(4)]

        def every_pass(eng, l, one_pass):
            with eng.Fori(0, PAIRS) as i:
                v = passes(eng, l, i)
                for j in range(2):
                    one_pass(j, v[2 * j])
                    with eng.If(v[2 * j + 1] > 1):
                        with eng.Fori(1, NB) as b:
                            with eng.If(v[2 * j + 1] > b):
                                one_pass(j, v[2 * j] + b)
                            eng.nop()
                        eng.nop()
                    eng.nop()

        def carry(eng):
            eng.sem_inc(S["carried"], 1)

        block = ctx.enter_context(nc.Block())

        @block.sync
        def _(sp):
            def load(s, src):
                sp.dma_start(ring[:, s, :].rearrange("p (k n) -> p k n", k=KD), src).then_inc(slot_in[s], 16)

            ada = a["w_ada"].rearrange("l (k p) n -> l p k n", p=P)
            with sp.Fori(0, 2) as l:
                with sp.Fori(0, 2) as h:
                    for s in range(NSLOT):
                        sp.wait_ge(slot_free[s], 2 * l + h)
                        load(s, ada[l, :, :, bass.ds(h * (3 * D) + 512 * s, 512)])
            wina = a["w_in_a"][0].rearrange("(k p) n -> p k n", p=P)
            for s, col in enumerate((3, 4, 0, 1, 2)):
                sp.wait_ge(slot_free[s], 4)
                load(s, wina[:, :, 512 * col:512 * col + 512])
            wouta = a["w_out_a"][0].rearrange("(k p) n -> p k n", p=P)
            sp.wait_ge(slot_free[5], 4)
            load(5, wouta[:, :, 0:512])
            sp.wait_ge(S["page_in"], 16)
            ck = a["cache_k"][0].rearrange("n r h d -> n r (h d)")
            cvd = a["cache_v"][0].rearrange("n r h d -> n r (h d)")
            sp.wait_ge(S["u_mm"], 4)
            sp.wait_ge(S["tok_mm"], 2 * NT)
            with sp.Fori(0, 4) as it:
                for s in range(4):
                    sp.wait_ge(S["page_in"], 16)
                    sp.wait_ge(slot_free[s], it + 4)
                    for g in range(NPG):
                        page = sp.value_load(pgt[0:1, bass.ds(it * (2 * NPG) + (s // 2) * NPG + g, 1)],
                                             min_val=0, max_val=a["cache_k"].shape[1] - 1)
                        sp.dma_start(ring[:, s, 512 * g:512 * g + 512],
                                     (ck if s % 2 == 0 else cvd)[page, :, :]).then_inc(slot_in[s], 16)
            sp.wait_ge(S["tok_mm"], 3 * NT)
            load(4, wouta[:, :, 512:1024])

            def experts(l):
                gu = a["w_gate_up"][l].rearrange("e (k p) n -> e p k n", p=P)
                dn = a["w_down"][l].rearrange("e (k p) n -> e p k n", p=P)

                def part(e, j, k):
                    src = gu[e, :, 4 * k:4 * k + 4, :] if k < 2 else dn[e, :, :, :]
                    sp.dma_start(ring[:, 3 * j + k, :].rearrange("p (k n) -> p k n", k=4), src).then_inc(
                        slot_in[3 * j + k], 16)

                for s in range(NSLOT):
                    if l == 0 and s < 4:
                        sp.wait_ge(slot_free[s], 8)
                    elif l == 0:
                        layer_wait(sp, 0, "wo_mm", NT if s == 5 else 2 * NT)
                    elif s < 2:
                        layer_wait(sp, 1, "wo_mm", NT * (s + 1))
                    else:
                        sp.wait_ge(S["bch_mm"], 4 * (s // 3 + 1))
                    part(s // 3, s // 3, s % 3)
                layer_wait(sp, l, "bounds", 1)
                with sp.Fori(1, PAIRS) as i:
                    before = [sp.value_load(tab[l][0:1, bass.ds(i, 1), 2 * j:2 * j + 1], min_val=0,
                                            max_val=2 * E * NB) for j in range(2)]
                    for j in range(2):
                        n = before[j]
                        sp.wait_ge(M[j]["gu_mm"], n)
                        part(2 * i + j, j, 0)
                        part(2 * i + j, j, 1)
                        sp.wait_ge(M[j]["down_mm"], n)
                        part(2 * i + j, j, 2)
                for j in range(2):
                    n = sp.value_load(tab[l][0:1, PAIRS:PAIRS + 1, 2 * j:2 * j + 1], min_val=0, max_val=2 * E * NB)
                    layer_wait(sp, l, "bounds", 1)
                    sp.wait_ge(M[j]["down_mm"], n)

            experts(0)
            winc = a["w_in_c"][0].rearrange("(k p) n -> p k n", p=P)
            for s in range(NSLOT):
                col = D * (s % 3) + 512 * (s // 3)
                load(s, winc[:, :, col:col + 512])
            woutc = a["w_out_c"][0].rearrange("(k p) n -> p k n", p=P)
            sp.wait_ge(S["bch_mm"], 4)
            for s in range(2):
                load(s, woutc[:, :, 512 * s:512 * s + 512])
            experts(1)

        @block.tensor
        def _(pe):
            mm, tr = nc.tensor.matmul, nc.tensor.transpose

            def tile8(s):
                return ring[:, s, :].rearrange("p (k n) -> p k n", k=KD)

            pe.wait_ge(S["params_in"], 16 * 26)
            tr(ps[:, 6, 0:96], W[0:96, 0:P], ident[0:96, 0:96])
            tr(ps[:, 6, 96:165], W[0:69, P:2 * P], ident[0:69, 0:69])
            tr(ps[:, 6, 165:289], W[0:124, 2 * P:3 * P], ident[0:124, 0:124]).then_inc(S["prm_tr"], 1)
            pe.wait_ge(S["c_silu"], 1)
            for c in range(KD):
                x = tr(ps[:, 7, 9 * c:9 * c + 9], W[0:9, W_C + P * c:W_C + P * c + P], ident[0:9, 0:9])
            x.then_inc(S["c_tr"], 1)
            pe.wait_ge(S["c_ev"], 1)
            with pe.Fori(0, 4) as it:
                for s in range(NSLOT):
                    pe.wait_ge(slot_in[s], 16 * it + 16)
                    if s == 0:
                        pe.wait_ge(S["ada_ev"], 2 * it)
                    for m in range(4):
                        at = 9 * (4 * (s % 3) + m)
                        for k in range(KD):
                            x = mm(ps[:, s // 3, at:at + 9], tile8(s)[:, k, P * m:P * m + P], cT[:, k, :],
                                   start=(k == 0), stop=(k == KD - 1))
                    x.then_inc(slot_free[s], 1)
            meet(pe, 0)

            def norm_transposes(l):
                layer_wait(pe, l, "xn_a", 2)
                layer_wait(pe, l, "xn_d", 3)
                for c in range(KD):
                    if c >= 4:
                        layer_wait(pe, l, "ev1a" if c % 2 == 0 else "ev1d", (c - 4) // 2 + 1)
                    for i in range(4):
                        x = tr(ps[:, c % 4, P * i:P * i + P], Hb[:, i, P * c:P * c + P], ident)
                    x.then_inc(L["tr1"], 1)
                for c in range(KD):
                    x = tr(ps[:, 4, NS * c:NS * c + NS], Hb[0:NS, LS, P * c:P * c + P], ident[0:NS, 0:NS])
                x.then_inc(L["tr1"], 1)
                layer_wait(pe, l, "ev1a", 4)
                layer_wait(pe, l, "ev1d", 5)

            def spread(l, n, src, b0, at=W_RA):
                for c in range(KD):
                    mm(ps[:, b0 + c // 4, P * (c % 4):P * (c % 4) + P], src[:, c, 0:1].to_broadcast([P, P]), ident,
                       start=True, stop=True)
                layer_wait(pe, l, "rep_ok", n)
                for c in range(KD):
                    x = mm(ps[0:NS, b0 + 2 + c // 4, P * (c % 4):P * (c % 4) + P], w(at, KD, NS)[:, c, :], ident,
                           start=True, stop=True)
                return x

            def out_proj(l, yT, slots, arrived):
                for n, s in enumerate(slots):
                    pe.wait_ge(slot_in[s], arrived[n])
                    for i in range(NT):
                        u = n * NT + i
                        if u >= 4:
                            layer_wait(pe, l, "wo_mul", u - 3)
                        for k in range(KD):
                            x = mm(ps[0:rows(i), u % 4, :], yT[:, k, toks(i)], tile8(s)[:, k, :],
                                   start=(k == 0), stop=(k == KD - 1))
                        x.then_inc(L["wo_mm"], 1)

            norm_transposes(0)
            pe.wait_ge(slot_in[0], 80)
            pe.wait_ge(slot_in[1], 80)
            for m in range(4):
                if m >= 2:
                    pe.wait_ge(S["u_ok"], 2 * (m - 1))
                for s in range(2):
                    ws = tile8(s)[:, :, P * m:P * m + P]
                    for k in range(KD):
                        mm(ps[:, 2 * (m % 2) + s, :], ws[:, k, :], hT[:, k, 0:TP], start=(k == 0), stop=(k == KD - 1))
                    for k in range(KD):
                        x = mm(ps[:, 4 + m % 2, NS * s:NS * s + NS], ws[:, k, :], hT[:, k, TP:T],
                               start=(k == 0), stop=(k == KD - 1))
                x.then_inc(S["u_mm"], 1)
            pe.wait_ge(S["u_state"], 32)
            for r in range(2):
                for c in range(4):
                    x = tr(ps[:, 6 + r, 120 * c:120 * c + 120], w(W_CV + 512 * r, 4, P, rows=120)[:, c, :],
                           ident[0:120, 0:120])
            x.then_inc(S["st_tr"], 1)
            pe.wait_ge(S["st_ev"], 2)
            pe.wait_ge(S["u_ok"], 8)
            for u in range(3 * NT):
                s, i = 2 + u // NT, u % NT
                if i == 0:
                    pe.wait_ge(slot_in[s], 80)
                if u >= 4:
                    pe.wait_ge(S["tok_copy"], u - 3)
                for k in range(KD):
                    x = mm(ps[0:rows(i), u % 4, :], hT[:, k, toks(i)], tile8(s)[:, k, :],
                           start=(k == 0), stop=(k == KD - 1))
                x.then_inc(S["tok_mm"], 1)
                v = u - 1
                if 0 <= v < 2 * NT:
                    r = rows(v % NT)
                    pe.wait_ge(S["tok_g"], v + 1)
                    if v >= 2:
                        pe.wait_ge(S["tok_ev"], v - 1)
                    for c in range(H):
                        x = tr(ps[:, 6 + v % 2, P * c:P * c + r], raw[0:r, v % 3, P * c:P * c + P], ident[0:r, 0:r])
                    x.then_inc(S["tok_tr"], 1)
            meet(pe, 1)
            for c in range(4):
                mm(ps[:, 0, :], ones, cv[:, c, 0:TP], start=(c == 0), stop=(c == 3))
            for c in range(4):
                x = mm(ps[:, 1, 0:NS], ones, cv[:, c, TP:T], start=(c == 0), stop=(c == 3))
            x.then_inc(S["ln_mm"], 1)
            pe.wait_ge(S["un_ok"], 1)
            for c in range(4):
                tr(ps[0:PAD, 6, P * c:P * c + P], uT[:, c, TP:TP + PAD], ident)
            for c in range(4):
                x = tr(ps[0:NS, 7, P * c:P * c + P], w(W_SG, 4, NS)[:, c, :], ident)
            x.then_inc(S["uo_tr"], 1)
            for c in range(4):
                pe.wait_ge(S["ln_sq"], c + 1)
                v = w(W_RAW, 2, T)[:, c % 2, :]
                mm(ps[:, 2, :], ones, v[:, 0:TP], start=(c == 0), stop=(c == 3), skip_group_check=True)
                x = mm(ps[:, 3, 0:NS], ones, v[:, TP:T], start=(c == 0), stop=(c == 3), skip_group_check=True)
                x.then_inc(S["ln_mm"], 1)
            meet(pe, 2)

            def scores(u):
                h, i = divmod(u, 4)
                if u >= 2:
                    pe.wait_ge(S["at_b"], 2 * (u - 1))
                for m in range(2):
                    x = mm(ps[:, 2 * (u % 2) + m, 0:P * (i + 1)], QT[HD * m:HD * m + HD, h, P * i:P * i + P],
                           KT[HD * m:HD * m + HD, h, 0:P * (i + 1)], start=True, stop=True)
                x.then_inc(S["at_s"], 1)

            scores(0)
            for u in range(4 * H):
                h, i = divmod(u, 4)
                if u + 1 < 4 * H:
                    scores(u + 1)
                pe.wait_ge(S["at_p"], u + 1)
                if u >= 2:
                    pe.wait_ge(S["at_pt"], u - 1)
                for c in range(i + 1):
                    x = tr(ps[:, 4 + u % 2, P * c:P * c + P], w(W_E, 4, 4, P)[:, 2 * (u % 2), c, :], ident)
                x.then_inc(S["at_tr"], 1)
                if i == 3:
                    pe.wait_ge(S["at_pt"], u + 1)
                    if h >= 2:
                        pe.wait_ge(S["at_ov"], h - 1)
                    for c in range(4):
                        x = mm(ps[:, 6 + h % 2, P * c:TP], V[:, c, P * h:P * h + P], w(W_PT, 4, TP)[:, c, P * c:TP],
                               start=(c == 0), stop=(c == 3), skip_group_check=True)
                    x.then_inc(S["at_o"], 1)
            meet(pe, 3)

            def key_turns(sk, q):
                for g in range(4):
                    at = 512 * (4 * (q // 4) + g) + P * (q % 4)
                    x = tr(ps[:, 3 + q % 2, P * g:P * g + P], ring[:, sk, at:at + P], ident)
                x.then_inc(S["sp_kt"], 1)

            with pe.Fori(0, 4) as it:
                for b in range(2):
                    sk, sv, n = 2 * b, 2 * b + 1, 2 * it + b
                    pe.wait_ge(slot_in[sk], seq * it + (seq + 80))
                    key_turns(sk, 0)
                    pe.wait_ge(S["sp_q"], n + 1)
                    pe.wait_ge(S["sp_d"], 8 * n)
                    for q in range(2 * H):
                        if q < 2 * H - 1:
                            key_turns(sk, q + 1)
                        pe.wait_ge(S["sp_eva" if q % 2 == 0 else "sp_evd"], 4 * n + (q // 2 + 1))
                        mm(ps[0:32, q // 4, :], w(W_QC, H, 32)[:, q % 4, :], w(W_KT, 2, 512)[:, q % 2, :],
                           start=(q % 4 == 0), stop=(q % 4 == H - 1), skip_group_check=True).then_inc(S["sp_s"], 1)
                    for h in range(H):
                        x = mm(ps[0:32, 2, 0:NS], w(W_QC, H, 32)[:, h, :], KT[:, h, TP:T],
                               start=(h == 0), stop=(h == H - 1))
                    x.then_inc(slot_free[sk], 1)
                    pe.wait_ge(S["sp_d"], 8 * n + 8)
                    for g in range(NPG + 1):
                        k = P if g < NPG else NS
                        x = mm(ps[0:k, 5, 16 * g:16 * g + 16], w(W_S, PAST + NS, rows=32)[:, P * g:P * g + k],
                               cmb[:, 16:32], start=True, stop=True)
                    x.then_inc(S["sp_pt"], 1)
                    pe.wait_ge(slot_in[sv], seq * it + (seq + 80))
                    pe.wait_ge(S["sp_ptev"], 2 * n + 2)
                    pe.wait_ge(S["sp_ov"], n)
                    pT = w(W_PS, NPG + 1, 16)
                    for h in range(H):
                        for g in range(NPG):
                            mm(ps[:, 6, TS * h:TS * h + TS], ring[:, sv, 512 * g + P * h:512 * g + P * h + P],
                               pT[:, g, TS * h:TS * h + TS], start=(g == 0), stop=False)
                        x = mm(ps[:, 6, TS * h:TS * h + TS], V[0:NS, LS, P * h:P * h + P],
                               pT[0:NS, NPG, TS * h:TS * h + TS], start=False, stop=True)
                    x.then_inc(slot_free[sv], 1)
            meet(pe, 4)
            for h in range(H):
                pe.wait_ge(S["on_sq"], h + 1)
                v = w(W_SQ, 2, T)[:, h % 2, :]
                mm(ps[:, h, :], ones, v[:, 0:TP], start=True, stop=True)
                mm(ps[:, 4, NS * h:NS * h + NS], ones, v[:, TP:T], start=True, stop=True).then_inc(S["on_mm"], 1)
            meet(pe, 5)
            spread(0, 1, mod(0, 2), 4).then_inc(L["gate_mm"], 1)
            out_proj(0, hT, (5, 4), (80, 96))
            meet(pe, 6)

            def ffn(l, k0):
                spread(l, 2, scT[:, 2 + l, :, :], 0)
                spread(l, 3, mod(l, 3), 4, W_RB).then_inc(L["bc_mm"], 1)
                layer_wait(pe, l, "bc_ev", 8)
                layer_wait(pe, l, "h_ok", NT)
                for c in range(KD):
                    if c >= 4:
                        layer_wait(pe, l, "ev2a" if c % 2 == 0 else "ev2d", (c - 4) // 2 + 1)
                    for i in range(4):
                        x = tr(ps[:, c % 4, P * i:P * i + P], Hb[:, i, P * c:P * c + P], ident)
                    x.then_inc(L["tr2"], 1)
                for c in range(KD):
                    x = tr(ps[:, 4, NS * c:NS * c + NS], Hb[0:NS, LS, P * c:P * c + P], ident[0:NS, 0:NS])
                x.then_inc(L["tr2"], 1)
                layer_wait(pe, l, "ev2a", 4)
                layer_wait(pe, l, "ev2d", 5)
                for i in range(NT):
                    for k in range(KD):
                        x = mm(ps[0:rows(i), 5, NR * i:NR * i + NR], hT[:, k, toks(i)], wr[:, l, k, :],
                               start=(k == 0), stop=(k == KD - 1))
                x.then_inc(L["lg_mm"], 1)
                layer_wait(pe, l, "r_ok", 1)
                cc = w(R_CC, NT, E)
                for i in range(NT):
                    for q in range(i + 1):
                        x = mm(ps[:, 6, E * i:E * i + E], upper if q == i else ones, cc[:, q, :],
                               start=(q == 0), stop=(q == i))
                for q in range(NT):
                    x = mm(ps[:, 6, E * NT:E * NT + E], ones, cc[:, q, :], start=(q == 0), stop=(q == NT - 1))
                x.then_inc(L["cnt_mm"], 1)
                for q in range(2 * NT):
                    layer_wait(pe, l, "oh_ok", q + 1)
                    for b in range(NB):
                        x = mm(ps[0:CAP, b // 5, 96 * (b % 5):96 * (b % 5) + 96],
                               w(W_OH, 2, NB * CAP)[:, q % 2, CAP * b:CAP * b + CAP], w(W_V3, 2 * NT, 96)[:, q, :],
                               start=(q == 0 and b % 5 == 0), stop=(q == 2 * NT - 1), skip_group_check=True)
                    x.then_inc(L["list_mm"], 1)
                meet(pe, k0)

                def one_pass(j, n, arrived):
                    m = M[j]
                    pe.wait_ge(m["gathered"], 16 * n + 16)
                    pe.wait_ge(m["xt_ok"], n)
                    carry(pe)
                    xg, xt = w(W_XG + D * j, KD, P, rows=CAP), w(W_XT + 512 * j, KD, CAP)
                    for k in range(KD):
                        x = tr(ps[:, j, CAP * k:CAP * k + CAP], xg[:, k, :], ident[0:CAP, 0:CAP])
                    x.then_inc(m["xt_mm"], 1)
                    if arrived is not None:
                        pe.wait_ge(slot_in[3 * j], arrived[0])
                        pe.wait_ge(slot_in[3 * j + 1], arrived[1])
                    pe.wait_ge(m["xt_ok"], n + 1)
                    pe.wait_ge(m["h_ok"], n)
                    for f in range(2 * FE // P):
                        for k in range(KD):
                            at = D * (k % 4) + P * f
                            x = mm(ps[:, 2 + j, CAP * f:CAP * f + CAP], ring[:, 3 * j + k // 4, at:at + P], xt[:, k, :],
                                   start=(k == 0), stop=(k == KD - 1))
                    x.then_inc(m["gu_mm"], 1)
                    if arrived is not None:
                        pe.wait_ge(slot_in[3 * j + 2], arrived[2])
                    pe.wait_ge(m["h_ok"], n + 1)
                    pe.wait_ge(m["ya_ok"], n)
                    pe.wait_ge(m["yd_ok"], n)
                    for z in range(2):
                        for k in range(FE // P):
                            x = mm(ps[0:CAP, 4 + 2 * j + z, :], w(W_HH + 256 * j, 4, CAP)[:, k, :],
                                   ring[:, 3 * j + 2, D * k + 512 * z:D * k + 512 * z + 512],
                                   start=(k == 0), stop=(k == FE // P - 1))
                    x.then_inc(m["down_mm"], 1)

                with pe.Fori(0, PAIRS) as i:
                    v = passes(pe, l, i)
                    for j in range(2):
                        one_pass(j, v[2 * j], [base_in[l][3 * j + q] + 16 + 16 * i for q in range(3)])
                        with pe.If(v[2 * j + 1] > 1):
                            with pe.Fori(1, NB) as b:
                                with pe.If(v[2 * j + 1] > b):
                                    one_pass(j, v[2 * j] + b, None)
                                pe.nop()
                            pe.nop()
                        pe.nop()
                meet(pe, k0 + 1)
                spread(l, 4, mod(l, 5), 4).then_inc(L["gate2_mm"], 1)

            ffn(0, 7)
            meet(pe, 9)
            norm_transposes(1)
            pe.wait_ge(S["vs_in"], 16)
            for c in range(KD):
                x = tr(ps[:, 7, 16 * c:16 * c + 16], w(W_ST, D, rows=16)[:, P * c:P * c + P], ident[0:16, 0:16])
            x.then_inc(S["vs_tr"], 1)
            pe.wait_ge(S["vs_ok"], 1)
            for c in range(KD):
                if c >= 2:
                    pe.wait_ge(S["z_ok"], c - 1)
                for s in range(3):
                    r = 3 * (c // 4) + s
                    if c % 4 == 0:
                        pe.wait_ge(slot_in[r], in0[r] + 16 * PAIRS + 16)
                    ws = tile8(r)[:, :, P * (c % 4):P * (c % 4) + P]
                    for k in range(KD):
                        mm(ps[:, 4 * (c % 2) + s, :], ws[:, k, :], hT[:, k, 0:TP], start=(k == 0), stop=(k == KD - 1))
                    for k in range(KD):
                        x = mm(ps[:, 4 * (c % 2) + 3, NS * s:NS * s + NS], ws[:, k, :], hT[:, k, TP:T],
                               start=(k == 0), stop=(k == KD - 1))
                x.then_inc(S["bch_mm"], 1)
            meet(pe, 10)
            for c in range(KD):
                tr(ps[0:2, c // 4, P * (c % 4):P * (c % 4) + P], vK[:, c, :], ident)
            for c in range(KD):
                x = tr(ps[0:NS, 2 + c // 4, P * (c % 4):P * (c % 4) + P], vN[:, c, :], ident)
            x.then_inc(S["vo_tr"], 1)
            spread(1, 1, mod(1, 2), 4).then_inc(L["gate_mm"], 1)
            pe.wait_ge(S["vo_ok"], 4)
            out_proj(1, zT, (0, 1), (in1[0], in1[1]))
            meet(pe, 11)
            ffn(1, 12)

        @block.scalar
        def _(act):
            fn = nc.scalar.activation

            def copy(out, src, **k):
                return fn(out, src, ACT.Copy, **k)

            def ld(dst, src):
                act.dma_start(dst, src).then_inc(S["params_in"], 16)

            ld(W[0:1, W_C:W_C + D], a["c_prompt"])
            ld(W[1:9, W_C:W_C + D], a["c_sample"])
            ld(C[:, :], a["consts"])
            ld(W[0:96, 0:P], a["b_ada"].rearrange("l (m p) -> (l m) p", p=P))
            at = 0
            for v in (a["norm_mix_g"].rearrange("l (c p) -> (l c) p", p=P), a["norm_ffn_g"].rearrange("l (c p) -> (l c) p", p=P),
                      a["convb_b"].rearrange("l (c p) -> (l c) p", p=P), a["convb_ln_g"].rearrange("l (c p) -> (l c) p", p=P),
                      a["convb_ln_b"].rearrange("l (c p) -> (l c) p", p=P), a["subln_g"],
                      a["convc_w"].rearrange("l w o (c p) -> (l w o c) p", p=P)):
                ld(W[at:at + v.shape[0], P:2 * P], v)
                at += v.shape[0]
            ld(W[0:124, 2 * P:3 * P], a["convb_w"].rearrange("l w o (c p) -> (l w o c) p", p=P))
            act.dma_start(X[:, 0:4, :], a["x_prompt"][0].rearrange("(i p) d -> p i d", p=P)).then_inc(S["x_in"], 16)
            act.dma_start(X[0:NS, LS, :], a["x_sample"].rearrange("s t d -> (s t) d")).then_inc(S["x_in"], 16)
            act.dma_start(pgt[:, :], a["page_table"].rearrange("s g -> (s g)").rearrange("(o n) -> o n", o=1)).then_inc(
                S["page_in"], 16)
            for q, n in enumerate(("q_norm_g", "k_norm_g")):
                ld(qkg[:, q, :], a[n].rearrange("l m d -> l (m d)").to_broadcast([P, P]))
            for q, n in enumerate(("lam_q1", "lam_k1", "lam_q2", "lam_k2")):
                ld(w(W_LAM, 4, HD)[:, q, :], a[n].to_broadcast([P, HD]))
            for l in range(2):
                ld(rb[:, l, 0:G], a["b_group"][l:l + 1, :].to_broadcast([P, G]))
                ld(rb[:, l, G:NR], a["b_router"][l:l + 1, :].to_broadcast([P, E]))
                ld(wr[:, l, :, 0:G], a["w_group"][l].rearrange("(k p) n -> p k n", p=P))
                ld(wr[:, l, :, G:NR], a["w_router"][l].rearrange("(k p) n -> p k n", p=P))
            act.wait_ge(S["params_in"], 16 * 26)
            fn(W[0:9, W_C:W_C + D], W[0:9, W_C:W_C + D], ACT.Silu).then_inc(S["c_silu"], 1)
            act.wait_ge(S["c_tr"], 1)
            copy(cT[:, :, :].rearrange("p c s -> p (c s)"), ps[:, 7, 0:9 * KD]).then_inc(S["c_ev"], 1)
            act.wait_ge(S["lam_sum"], 1)
            fn(lamw[:, 2:4], lamw[:, 0:2], ACT.Exp).then_inc(S["lam_exp"], 1)

            def root(out, src, n):
                return fn(out, src, ACT.Sqrt, scale=1.0 / n, bias=epsc[0:src.shape[0], :])

            def rms(l, r):
                for i in range(NT):
                    fn(Hb[0:rows(i), i, :], X[0:rows(i), i, :], ACT.Square,
                       accum_out=st[0:rows(i), i:i + 1]).then_inc(L[f"rms{r}_sum"], 1)
                layer_wait(act, l, f"rms{r}_sum", NT)
                root(st[:, 8:8 + NT], st[:, 0:NT], D).then_inc(L[f"rms{r}_root"], 1)

            def norm(l):
                rms(l, 1)
                layer_wait(act, l, "rms1_inv", 1)
                for i in range(2):
                    fn(Hb[:, i, :], X[:, i, :], ACT.Copy, scale=st[:, 16 + i:17 + i]).then_inc(L["xn_a"], 1)

            def norm_ev(l):
                for c in range(0, KD, 2):
                    layer_wait(act, l, "tr1", c + 1)
                    fn(hT[:, c, 0:TP], ps[:, c % 4, :], ACT.Identity, scale=scT[:, l, c, 0:1],
                       bias=mod(l, 0)[:, c, 0:1]).then_inc(L["ev1a"], 1)

            def gates(l, name):
                layer_wait(act, l, name + "_mm", 1)
                for z in range(2):
                    copy(w(W_G + 512 * z, 512), ps[:, 4 + z, :]).then_inc(L[name + "_ev"], 1)
                    copy(w(W_GS + 512 * z, 512, rows=NS), ps[0:NS, 6 + z, :]).then_inc(L[name + "_ev"], 1)

            act.wait_ge(S["x_in"], 32)
            act.wait_ge(S["stats_set"], 1)
            norm(0)
            meet(act, 0)
            for r in range(2):
                act.dma_start(w(W_CV + 512 * r, 512, rows=120),
                              a["state_conv_b"][0, 4 * r:4 * r + 4].rearrange("s t c -> (s t) c")).then_inc(S["u_state"], 16)
            norm_ev(0)
            for m in range(4):
                act.wait_ge(S["u_mm"], m + 1)
                if m >= 1:
                    act.wait_ge(S["u_ok"], 2 * m)
                fn(sg[:, 0:TP], ps[:, 2 * (m % 2) + 1, :], ACT.Sigmoid).then_inc(S["u_sig"], 1)
                fn(sg[:, TP:T], ps[:, 4 + m % 2, NS:2 * NS], ACT.Sigmoid).then_inc(S["u_sig"], 1)

            def tok_ev(v):
                i, r = v % NT, rows(v % NT)
                act.wait_ge(S["tok_tr"], v + 1)
                fn((QT if v < NT else KT)[:, :, toks(i)], bank(6 + v % 2, H, P)[:, :, 0:r], ACT.Copy,
                   scale=HD ** -0.5 if v < NT else 1.0).then_inc(S["tok_ev"], 1)

            for u in range(3 * NT):
                i, r = u % NT, rows(u % NT)
                act.wait_ge(S["tok_mm"], u + 1)
                if u >= 2 * NT:
                    copy(V[0:r, i, :], ps[0:r, u % 4, :]).then_inc(S["tok_copy"], 1)
                    if u == 2 * NT:
                        tok_ev(u - 1)
                    continue
                if u >= 3:
                    act.wait_ge(S["tok_tr"], u - 2)
                if u - 3 >= NT:
                    act.wait_ge(S["kv_out"], 16 * (u - 3 - NT + 1))
                copy(raw[0:r, u % 3, :], ps[0:r, u % 4, :]).then_inc(S["tok_copy"], 1)
                act.wait_ge(S["tok_copy"], u + 1)
                if u >= 1:
                    act.wait_ge(S["tok_ss"], u)
                fn(sq[0:r, :], raw[0:r, u % 3, :], ACT.Square).then_inc(S["tok_sq"], 1)
                act.wait_ge(S["tok_ss"], u + 1)
                root(st[0:r, 32:40], st[0:r, 24:32], HD).then_inc(S["tok_root"], 1)
                if u >= 1:
                    tok_ev(u - 1)
            meet(act, 1)
            act.wait_ge(S["uo_tr"], 1)
            so = hT[:, :, :].rearrange("p c t -> p (c t)")
            copy(so[0:PAD, 0:512], ps[0:PAD, 6, :]).then_inc(S["uo_ev"], 1)
            copy(so[0:NS, 512:1024], ps[0:NS, 7, :]).then_inc(S["uo_ev"], 1)
            for c in range(4):
                act.wait_ge(S["ln_x"], 2 * c + 2)
                if c >= 2:
                    act.wait_ge(S["ln_mm"], c)
                fn(w(W_RAW, 2, T)[:, c % 2, :], cv[:, c, :], ACT.Square).then_inc(S["ln_sq"], 1)
            act.wait_ge(S["ln_mm"], 5)
            root(sg[:, 0:TP], ps[:, 2, :], 512).then_inc(S["ln_root"], 1)
            root(sg[:, TP:T], ps[:, 3, 0:NS], 512).then_inc(S["ln_root"], 1)
            for c in range(4):
                act.wait_ge(S["ln_n"], c + 1)
                fn(hT[:, 4 + c, :], cv[:, c, :], ACT.Silu, scale=lng[:, c:c + 1], bias=lnb[:, c:c + 1])
            act.wait_ge(S["uo_ev"], 2)
            act.dma_start(o["conv_b_prompt"][0, 0], so[0:PAD, 0:512]).then_inc(S["out_dma"], 16)
            act.dma_start(o["conv_b_sample"][0, :, 0:PAD - TS, :], a["state_conv_b"][0, :, TS:PAD, :]).then_inc(
                S["out_dma"], 16)
            for s in range(NSEQ):
                act.dma_start(o["conv_b_sample"][0, s, PAD - TS:PAD, :], so[TS * s:TS * s + TS, 512:1024]).then_inc(
                    S["out_dma"], 16)
            act.wait_ge(S["out_dma"], 160)
            meet(act, 2)
            act.dma_start(w(0, H * TP), a["prompt_bias"]).then_inc(S["bias_in"], 16)
            e = w(W_E, 4, TP)

            def exps(u):
                n = P * (u % 4 + 1)
                act.wait_ge(S["at_m"], u + 1)
                for m in range(2):
                    fn(e[:, 2 * (u % 2) + m, 0:n], e[:, 2 * (u % 2) + m, 0:n], ACT.Exp, bias=st[:, 4 * (u % 2) + 2 + m:4 * (u % 2) + 3 + m],
                       accum_out=st[:, 8 + 2 * (u % 2) + m:9 + 2 * (u % 2) + m]).then_inc(S["at_e"], 1)

            exps(0)
            for u in range(4 * H):
                h, i = divmod(u, 4)
                if u + 1 < 4 * H:
                    exps(u + 1)
                act.wait_ge(S["at_tr"], u + 1)
                if i == 0 and h >= 1:
                    act.wait_ge(S["at_o"], h)
                copy(w(W_PT, 4, TP)[:, 0:i + 1, P * i:P * i + P], bank(4 + u % 2, i + 1, P)).then_inc(S["at_pt"], 1)
                if i == 3:
                    act.wait_ge(S["at_o"], h + 1)
                    copy(hT[:, h, 0:TP], ps[:, 6 + h % 2, :]).then_inc(S["at_ov"], 1)
            meet(act, 3)
            act.dma_start(w(0, PAST + NSEQ * NS, rows=32), a["sample_bias"]).then_inc(S["bias_in"], 16)
            with act.Fori(0, 4) as it:
                for b in range(2):
                    n = 2 * it + b
                    for q in range(0, 2 * H, 2):
                        act.wait_ge(S["sp_kt"], 8 * n + (q + 1))
                        act.wait_ge(S["sp_s"], 8 * n + max(q - 1, 0))
                        copy(w(W_KT, 2, 512)[:, 0, :], ps[:, 3, :]).then_inc(S["sp_eva"], 1)
                    act.wait_ge(S["sp_d"], 8 * n + 6)
                    fn(w(W_S, PAST + NS, rows=32), w(W_S, PAST + NS, rows=32), ACT.Exp, bias=st[0:32, 5:6],
                       accum_out=st[0:32, 6:7]).then_inc(S["sp_e"], 1)
                    act.wait_ge(S["sp_pt"], n + 1)
                    copy(w(W_PS, 16 * NPG), ps[:, 5, 0:16 * NPG]).then_inc(S["sp_ptev"], 1)
                    copy(w(W_PS + 16 * NPG, 16, rows=NS), ps[0:NS, 5, 16 * NPG:16 * NPG + 16]).then_inc(S["sp_ptev"], 1)
            meet(act, 4)
            for h in range(H):
                if h >= 2:
                    act.wait_ge(S["on_mm"], h - 1)
                fn(w(W_SQ, 2, T)[:, h % 2, :], hT[:, h, :], ACT.Square).then_inc(S["on_sq"], 1)
            act.wait_ge(S["on_mm"], H)
            rn = w(W_RN, H, T)
            for h in range(H):
                root(rn[:, h, 0:TP], ps[:, h, :], 2 * HD).then_inc(S["on_root"], 1)
            root(rn[:, :, TP:T], bank(4, H, NS), 2 * HD).then_inc(S["on_root"], 1)
            meet(act, 5)
            gates(0, "gate")
            meet(act, 6)

            def ffn(l, k0):
                act.dma_start(w(W_SLOT, NB * CAP), a["slot_numbers"]).then_inc(L["slots_in"], 16)
                rms(l, 2)
                layer_wait(act, l, "bc_mm", 1)
                for n, at in enumerate((W_AP, W_AS, W_BP, W_BS)):
                    r = NS if n % 2 else P
                    for z in range(2):
                        copy(w(at + 512 * z, 512, rows=r), ps[0:r, 2 * n + z, :]).then_inc(L["bc_ev"], 1)
                for i in range(NT):
                    layer_wait(act, l, "h_ok", i + 1)
                    act.dma_start(h_dram[toks(i), :], Hb[0:rows(i), i, :]).then_inc(L["h_out"], 16)
                for c in range(0, KD, 2):
                    layer_wait(act, l, "tr2", c + 1)
                    copy(hT[:, c, 0:TP], ps[:, c % 4, :]).then_inc(L["ev2a"], 1)
                layer_wait(act, l, "r_dif", 1)
                fn(st[:, 56:76], st[:, 56:76], ACT.Exp)
                fn(st[:, 76:81], st[:, 76:81], ACT.Exp).then_inc(L["r_exp"], 1)
                layer_wait(act, l, "h_out", 16 * NT)
                meet(act, k0)

                def one_pass(j, n):
                    m = M[j]
                    act.wait_ge(m["xt_mm"], n + 1)
                    act.wait_ge(m["gu_mm"], n)
                    copy(w(W_XT + 512 * j, 512), ps[:, j, :]).then_inc(m["xt_ok"], 1)
                    act.wait_ge(m["gu_mm"], n + 1)
                    act.wait_ge(m["h_ok"], n)
                    fn(w(W_GT + 256 * j, 256), ps[:, 2 + j, 0:256], ACT.Silu).then_inc(m["silu_ok"], 1)
                    act.wait_ge(m["down_mm"], n + 1)
                    act.wait_ge(m["scattered"], 16 * n)
                    fn(w(W_Y + D * j, 512, rows=CAP), ps[0:CAP, 4 + 2 * j, :], ACT.Copy, scale=wj[j][:, :]).then_inc(
                        m["ya_ok"], 1)

                every_pass(act, l, one_pass)
                meet(act, k0 + 1)
                yv = y_dram.rearrange("(t k) d -> t (k d)", k=2)
                for i in range(2):
                    act.dma_start(w(W_YB, 2, 2 * D, rows=rows(i))[:, i % 2, :], yv[toks(i), :]).then_inc(L[f"y_in{i % 2}"], 16)
                gates(l, "gate2")
                for i in range(2, NT):
                    layer_wait(act, l, "y_add", i - 1)
                    act.dma_start(w(W_YB, 2, 2 * D, rows=rows(i))[:, i % 2, :], yv[toks(i), :]).then_inc(L[f"y_in{i % 2}"], 16)

            ffn(0, 7)
            meet(act, 9)
            act.dma_start(w(W_ST, D, rows=16), a["state_conv_c"][0].rearrange("s t c -> (s t) c")).then_inc(S["vs_in"], 16)
            norm(1)
            norm_ev(1)
            for c in range(KD):
                act.wait_ge(S["bch_mm"], c + 1)
                if c >= 2:
                    act.wait_ge(S["z_ok"], c - 1)
                g = w(W_CG, 2, T)[:, c % 2, :]
                copy(g[:, 0:TP], ps[:, 4 * (c % 2) + 1, :]).then_inc(S["cg_ok"], 1)
                copy(g[:, TP:T], ps[:, 4 * (c % 2) + 3, NS:2 * NS]).then_inc(S["cg_ok"], 1)
            meet(act, 10)
            act.wait_ge(S["vo_tr"], 1)
            for z in range(2):
                copy(w(W_SO + 512 * z, 512, rows=2), ps[0:2, z, :]).then_inc(S["vo_ok"], 1)
                copy(w(W_ST + 512 * z, 512, rows=NS), ps[0:NS, 2 + z, :]).then_inc(S["vo_ok"], 1)
            act.wait_ge(S["vo_ok"], 4)
            act.dma_start(o["conv_c_prompt"][0, 0], w(W_SO, D, rows=2)).then_inc(S["out_dma"], 16)
            for s in range(NSEQ):
                act.dma_start(o["conv_c_sample"][0, s], W[TS * s + 2:TS * s + 4, W_ST:W_ST + D]).then_inc(S["out_dma"], 16)
            gates(1, "gate")
            act.wait_ge(S["out_dma"], 160 + 144)
            meet(act, 11)
            ffn(1, 12)
            for i in range(NT):
                layer_wait(act, 1, "y_add", i + 1)
                dst = o["y_prompt"][0, toks(i), :] if i < LS else o["y_sample"].rearrange("s t d -> (s t) d")
                act.dma_start(dst, X[0:rows(i), i, :]).then_inc(S["out_dma"], 16)
            act.wait_ge(S["out_dma"], 304 + 16 * NT)

        @block.vector
        def _(dve):
            v = nc.vector
            link = linker(dve, "dve")
            tt, ts, stt = v.tensor_tensor, v.tensor_scalar, v.scalar_tensor_tensor

            def b3(x, n):
                return x.unsqueeze(len(x.shape)).to_broadcast(list(x.shape) + [n])

            v.memset(st[:, :], 1.0).then_inc(S["stats_set"], 1)
            dve.wait_ge(S["params_in"], 16 * 26)
            lv = w(W_LAM, 4, HD)
            for q in range(2):
                link(tt(lv[:, 2 * q, :], lv[:, 2 * q, :], lv[:, 2 * q + 1, :], ALU.mult))
                link(v.tensor_reduce(lamw[:, q:q + 1], lv[:, 2 * q, :], AX, ALU.add))
            link(v.tensor_copy(lamw[:, 5:6], lamw[:, 1:2]))
            v.tensor_copy(lamw[:, 6:7], lamw[:, 0:1]).then_inc(S["lam_sum"], 1)
            dve.wait_ge(S["lam_exp"], 1)
            link(stt(out=neglam, in0=lamw[:, 3:4], scalar=-LAM_INIT, in1=lamw[:, 2:3], op0=ALU.add, op1=ALU.subtract))
            link(stt(out=cmb[:, 0:16], in0=C[0:32, C_SEL + 16:C_SEL + 32], scalar=lamw[0:32, 4:5],
                     in1=C[0:32, C_SEL:C_SEL + 16], op0=ALU.mult, op1=ALU.add))
            dve.wait_ge(S["prm_tr"], 1)
            link(v.tensor_copy(prm[:, :], ps[:, 6, 0:289]))
            link(ts(subg, subg, 1.0 - LAM_INIT, None, ALU.mult))

            def norm(l):
                layer_wait(dve, l, "rms1_root", 1)
                v.reciprocal(st[:, 16:16 + NT], st[:, 8:8 + NT]).then_inc(L["rms1_inv"], 1)
                layer_wait(dve, l, "rms1_inv", 1)
                for i in range(2, NT):
                    ts(Hb[0:rows(i), i, :], X[0:rows(i), i, :], st[0:rows(i), 16 + i:17 + i], None,
                       ALU.mult).then_inc(L["xn_d"], 1)

            norm(0)
            with dve.Fori(0, 4) as it:
                for hb in range(2):
                    dve.wait_ge(slot_free[2 + 3 * hb], it + 1)
                    tt(modT[:, bass.ds(it * 24 + 12 * hb, 12), :], bank(hb, 12, 9),
                       b3(bT[:, bass.ds(it * 24 + 12 * hb, 12)], 9), ALU.add).then_inc(S["ada_ev"], 1)
            dve.wait_ge(S["ada_ev"], 8)
            for n in range(4):
                link(stt(out=scT[:, n, :, :], in0=mod(n % 2, 1 if n < 2 else 4), scalar=1.0, in1=b3(gT[:, n, :], 9),
                         op0=ALU.add, op1=ALU.mult))
            meet(dve, 0)

            def norm_ev(l):
                for c in range(1, KD, 2):
                    layer_wait(dve, l, "tr1", c + 1)
                    ts(hT[:, c, 0:TP], ps[:, c % 4, :], scT[:, l, c, 0:1], mod(l, 0)[:, c, 0:1], ALU.mult,
                       ALU.add).then_inc(L["ev1d"], 1)
                layer_wait(dve, l, "tr1", KD + 1)
                hs = hT[:, :, TP:T].rearrange("p c (s t) -> p c s t", t=TS)
                link(tt(hs, bank(4, KD, NSEQ, TS), b3(scT[:, l, :, 1:9], TS), ALU.mult))
                tt(hs, hs, b3(mod(l, 0)[:, :, 1:9], TS), ALU.add).then_inc(L["ev1d"], 1)

            link(v.memset(uT[:, :, 0:PAD], 0.0))
            norm_ev(0)
            for m in range(4):
                dve.wait_ge(S["u_sig"], 2 * m + 2)
                tt(uT[:, m, PAD:PAD + TP], ps[:, 2 * (m % 2), :], sg[:, 0:TP], ALU.mult).then_inc(S["u_ok"], 1)
                tt(uS[:, m, :, PAD:PAD + TS], bank(4 + m % 2, NSEQ, TS), sg[:, TP:T].rearrange("p (s t) -> p s t", t=TS),
                   ALU.mult).then_inc(S["u_ok"], 1)
            dve.wait_ge(S["st_tr"], 1)
            for r in range(2):
                v.tensor_copy(uS[:, :, 4 * r:4 * r + 4, 0:PAD], bank(6 + r, 4, 4, PAD)).then_inc(S["st_ev"], 1)
            dve.wait_ge(S["st_ev"], 2)
            dve.wait_ge(S["u_ok"], 8)

            def conv_tap(n):
                k, c = divmod(n, 4)
                if n >= 4:
                    dve.wait_ge(S["conv"], n - 3)
                if k == 0:
                    x = ts(cv[:, c, 0:TP], uT[:, c, 0:TP], cbw[:, 0, c:c + 1], cbb[:, c:c + 1], ALU.mult, ALU.add)
                else:
                    x = stt(out=cv[:, c, 0:TP], in0=uT[:, c, k:k + TP], scalar=cbw[:, k, c:c + 1], in1=cv[:, c, 0:TP],
                            op0=ALU.mult, op1=ALU.add)
                x.then_inc(S["conv"], 1)

            per = -(-4 * BW // (2 * NT))
            for u in range(2 * NT):
                r = rows(u % NT)
                dve.wait_ge(S["tok_sq"], u + 1)
                v.tensor_reduce(st[0:r, 24:32], sq[0:r, :].rearrange("p (g d) -> p g d", d=HD), AX, ALU.add).then_inc(
                    S["tok_ss"], 1)
                dve.wait_ge(S["tok_root"], u + 1)
                link(v.reciprocal(st[0:r, 40:48], st[0:r, 32:40]))
                rv = raw[0:r, u % 3, :].rearrange("p (g d) -> p g d", d=HD)
                tt(rv, rv, b3(st[0:r, 40:48], HD), ALU.mult).then_inc(S["tok_n"], 1)
                for n in range(per * u, min(per * u + per, 4 * BW)):
                    conv_tap(n)
            for c in range(4):
                for t in range(TS):
                    tmp = sg[:, 0:NSEQ * BW].rearrange("p (s k) -> p s k", k=BW)
                    link(tt(tmp, uS[:, c, :, t:t + BW], cbw[:, :, c].unsqueeze(1).to_broadcast([P, NSEQ, BW]), ALU.mult))
                    link(v.tensor_reduce(cv[:, c, TP + t:T:TS], tmp, AX, ALU.add))
                link(ts(cv[:, c, TP:T], cv[:, c, TP:T], cbb[:, c:c + 1], None, ALU.add))
            meet(dve, 1)
            v.tensor_copy(w(W_SG, 4, NSEQ, TS), uS[:, :, :, PAD:PAD + TS]).then_inc(S["un_ok"], 1)
            dve.wait_ge(S["ln_mm"], 1)
            for c in range(4):
                stt(out=cv[:, c, 0:TP], in0=ps[:, 0, :], scalar=-1.0 / 512, in1=cv[:, c, 0:TP], op0=ALU.mult,
                    op1=ALU.add).then_inc(S["ln_x"], 1)
                stt(out=cv[:, c, TP:T], in0=ps[:, 1, 0:NS], scalar=-1.0 / 512, in1=cv[:, c, TP:T], op0=ALU.mult,
                    op1=ALU.add).then_inc(S["ln_x"], 1)
            dve.wait_ge(S["ln_root"], 2)
            link(v.reciprocal(sg, sg))
            for c in range(4):
                tt(cv[:, c, :], cv[:, c, :], sg, ALU.mult).then_inc(S["ln_n"], 1)
            meet(dve, 2)
            dve.wait_ge(S["bias_in"], 16)
            e = w(W_E, 4, TP)
            bias = w(0, H, TP)

            def maxima(u):
                h, i = divmod(u, 4)
                n, s = P * (i + 1), 4 * (u % 2)
                dve.wait_ge(S["at_s"], u + 1)
                if u >= 2:
                    dve.wait_ge(S["at_tr"], u - 1)
                for m in range(2):
                    v.tensor_tensor_reduce(out=e[:, 2 * (u % 2) + m, 0:n], in0=ps[:, 2 * (u % 2) + m, 0:n],
                                           in1=bias[:, h, TP - n:TP], scale=1.0, scalar=-3e38, op0=ALU.add, op1=ALU.max,
                                           accum_out=st[:, s + m:s + m + 1]).then_inc(S["at_b"], 1)
                dve.wait_ge(S["at_b"], 2 * u + 2)
                ts(st[:, s + 2:s + 4], st[:, s:s + 2], -1.0, None, ALU.mult).then_inc(S["at_m"], 1)

            maxima(0)
            for u in range(4 * H):
                n = P * (u % 4 + 1)
                if u + 1 < 4 * H:
                    maxima(u + 1)
                dve.wait_ge(S["at_e"], 2 * u + 2)
                at = 12 + 2 * (u % 2)
                link(v.reciprocal(st[:, at:at + 2], st[:, 8 + 2 * (u % 2):10 + 2 * (u % 2)]))
                link(ts(st[:, 16:17], st[:, at + 1:at + 2], neglam, None, ALU.mult))
                e0, e1 = e[:, 2 * (u % 2), 0:n], e[:, 2 * (u % 2) + 1, 0:n]
                link(ts(e1, e1, st[:, 16:17], None, ALU.mult))
                stt(out=e0, in0=e0, scalar=st[:, at:at + 1], in1=e1, op0=ALU.mult, op1=ALU.add).then_inc(S["at_p"], 1)
            meet(dve, 3)
            qb = w(W_QB, NSEQ, H, 32)
            link(v.memset(qb, 0.0))
            for h in range(H):
                for m in range(2):
                    link(v.tensor_copy(qb[HD * m:HD * m + HD, :, h, 8 * h + 4 * m:8 * h + 4 * m + 4],
                                       QT[HD * m:HD * m + HD, h, TP:T].rearrange("p (s t) -> p s t", t=TS)))
            dve.wait_ge(S["bias_in"], 32)
            sb_ = w(W_S, PAST + NS, rows=32)
            bs = w(0, PAST + NSEQ * NS, rows=32)
            with dve.Fori(0, 4) as it:
                for b in range(2):
                    n = 2 * it + b
                    dve.wait_ge(slot_free[2 - 2 * b], it + (4 + b))
                    v.tensor_copy(w(W_QC, 4 * 32), qb.rearrange("p s h c -> p s (h c)")[:, bass.ds(n, 1), :].rearrange(
                        "p o c -> p (o c)")).then_inc(S["sp_q"], 1)
                    for q in range(1, 2 * H, 2):
                        dve.wait_ge(S["sp_kt"], 8 * n + (q + 1))
                        dve.wait_ge(S["sp_s"], 8 * n + (q - 1))
                        v.tensor_copy(w(W_KT, 2, 512)[:, 1, :], ps[:, 4, :]).then_inc(S["sp_evd"], 1)
                    dve.wait_ge(slot_free[2 * b], it + 5)
                    dve.wait_ge(S["sp_pt"], n)
                    carry(dve)
                    for half in range(2):
                        v.tensor_tensor_reduce(out=sb_[:, 512 * half:512 * half + 512], in0=ps[0:32, half, :],
                                               in1=bs[:, 512 * half:512 * half + 512], scale=1.0, scalar=-3e38,
                                               op0=ALU.add, op1=ALU.max, accum_out=st[0:32, half:half + 1]).then_inc(S["sp_d"], 1)
                    tt(sb_[:, PAST:PAST + NS], ps[0:32, 2, 0:NS], bs[:, bass.ds(n * NS + PAST, NS)], ALU.add).then_inc(
                        S["sp_d"], 1)
                    dve.wait_ge(S["sp_d"], 8 * n + 3)
                    v.tensor_reduce(st[0:32, 2:3], sb_[:, PAST:PAST + NS], AX, ALU.max).then_inc(S["sp_d"], 1)
                    dve.wait_ge(S["sp_d"], 8 * n + 4)
                    v.tensor_reduce(st[0:32, 4:5], st[0:32, 0:3], AX, ALU.max).then_inc(S["sp_d"], 1)
                    dve.wait_ge(S["sp_d"], 8 * n + 5)
                    ts(st[0:32, 5:6], st[0:32, 4:5], -1.0, None, ALU.mult).then_inc(S["sp_d"], 1)
                    dve.wait_ge(S["sp_e"], n + 1)
                    v.reciprocal(st[0:32, 7:8], st[0:32, 6:7]).then_inc(S["sp_d"], 1)
                    dve.wait_ge(S["sp_d"], 8 * n + 7)
                    ts(cmb[:, 16:32], cmb[:, 0:16], st[0:32, 7:8], None, ALU.mult).then_inc(S["sp_d"], 1)
                    dve.wait_ge(slot_free[2 * b + 1], it + 5)
                    v.tensor_copy(hT[:, 0:H, bass.ds(n * TS + TP, TS)], bank(6, H, TS)).then_inc(S["sp_ov"], 1)
            meet(dve, 4)
            dve.wait_ge(S["on_root"], H + 1)
            rn = w(W_RN, H, T)
            link(v.reciprocal(rn, rn))
            for h in range(H):
                stt(out=hT[:, h, :], in0=hT[:, h, :], scalar=subg, in1=rn[:, h, :], op0=ALU.mult,
                    op1=ALU.mult).then_inc(S["on_ok"], 1)
            meet(dve, 5)

            def repeat(src, at=W_RA):
                v.tensor_copy(w(at, KD, NSEQ, TS), b3(src[:, :, 1:9], TS)).then_inc(L["rep_ok"], 1)

            def out_mul(l):
                repeat(mod(l, 2))
                layer_wait(dve, l, "gate_ev", 4)
                for u in range(2 * NT):
                    z, i = divmod(u, NT)
                    layer_wait(dve, l, "wo_mm", u + 1)
                    if u >= 2:
                        layer_wait(dve, l, "wo_add", u - 1)
                    tt(w(W_YB, 2, 512, rows=rows(i))[:, u % 2, :], ps[0:rows(i), u % 4, :],
                       w((W_G if i < LS else W_GS) + 512 * z, 512, rows=rows(i)), ALU.mult).then_inc(L["wo_mul"], 1)

            out_mul(0)
            meet(dve, 6)

            def ffn(l, k0):
                repeat(scT[:, 2 + l, :, :])
                repeat(mod(l, 3), W_RB)
                layer_wait(dve, l, "rms2_root", 1)
                link(v.reciprocal(st[:, 16:16 + NT], st[:, 8:8 + NT]))
                layer_wait(dve, l, "bc_ev", 8)
                for i in range(NT):
                    stt(out=Hb[0:rows(i), i, :], in0=X[0:rows(i), i, :], scalar=st[0:rows(i), 16 + i:17 + i],
                        in1=w(W_AP if i < LS else W_AS, D, rows=rows(i)), op0=ALU.mult, op1=ALU.mult).then_inc(
                        L["h_mul"], 1)
                for c in range(1, KD, 2):
                    layer_wait(dve, l, "tr2", c + 1)
                    v.tensor_copy(hT[:, c, 0:TP], ps[:, c % 4, :]).then_inc(L["ev2d"], 1)
                layer_wait(dve, l, "tr2", KD + 1)
                v.tensor_copy(hT[:, :, TP:T], bank(4, KD, NS)).then_inc(L["ev2d"], 1)

                lg = w(R_LG, NT, NR)
                me, a1, a2, cc, t1, m2 = (w(x, NT, E) for x in (R_ME, R_A1, R_A2, R_CC, R_T, R_M2))
                i32, i32m, grpm = (C[:, x:x + E].unsqueeze(1).to_broadcast([P, NT, E]) for x in (C_I32, C_I32M, C_GRPM))
                valid = C[:, C_VALID:C_VALID + NT]
                link(v.memset(lg, 0.0))
                layer_wait(dve, l, "lg_mm", 1)
                link(tt(lg[:, 0:LS, :], bank(5, LS, NR), rb[:, l:l + 1, :].to_broadcast([P, LS, NR]), ALU.add))
                link(tt(lg[0:NS, LS, :], ps[0:NS, 5, NR * LS:NR * NT], rb[0:NS, l, :], ALU.add))
                gm, gi, v1, v2, i1 = (st[:, x:x + NT] for x in (24, 29, 34, 39, 44))
                tg = t1[:, :, 0:G]
                link(v.tensor_reduce(gm, lg[:, :, 0:G], AX, ALU.max))
                link(tt(tg, lg[:, :, 0:G], b3(gm, G), ALU.is_equal))
                link(stt(out=tg, in0=tg, scalar=-99.0, in1=C[:, C_I32:C_I32 + G].unsqueeze(1).to_broadcast([P, NT, G]),
                         op0=ALU.mult, op1=ALU.add))
                link(v.tensor_reduce(gi, tg, AX, ALU.min))
                link(tt(t1, grpm, b3(gi, E), ALU.is_equal))
                link(ts(t1, t1, -1.0, BIG, ALU.add, ALU.mult))
                link(tt(me, lg[:, :, G:NR], t1, ALU.add))
                for src, top, hot in ((me, v1, a1), (m2, v2, a2)):
                    link(v.tensor_reduce(top, src, AX, ALU.max))
                    link(tt(t1, src, b3(top, E), ALU.is_equal))
                    link(stt(out=t1, in0=t1, scalar=-99.0, in1=i32, op0=ALU.mult, op1=ALU.add))
                    link(v.tensor_reduce(i1, t1, AX, ALU.min))
                    link(tt(hot, i32m, b3(i1, E), ALU.is_equal))
                    if src is me:
                        link(stt(out=m2, in0=hot, scalar=-3e38, in1=me, op0=ALU.mult, op1=ALU.add))
                for hot in (a1, a2):
                    link(tt(hot, hot, b3(valid, E), ALU.mult))
                link(tt(cc, a1, a2, ALU.add))
                link(tt(st[:, 56:76].rearrange("p (i g) -> p i g", g=G), lg[:, :, 0:G], b3(gm, G), ALU.subtract))
                link(tt(st[:, 76:81], v2, v1, ALU.subtract))
                v.tensor_copy(st[:, 86:87], st[:, 80:81]).then_inc(L["r_dif"], 1)
                v.tensor_copy(st[:, 87:88], st[:, 24:25]).then_inc(L["r_ok"], 1)
                layer_wait(dve, l, "r_exp", 1)
                gs, w1, w2 = st[:, 81:86], st[:, 49:54], st[:, 88:93]
                link(v.tensor_reduce(gs, st[:, 56:76].rearrange("p (i g) -> p i g", g=G), AX, ALU.add))
                link(stt(out=w1, in0=st[:, 76:81], scalar=1.0, in1=gs, op0=ALU.add, op1=ALU.mult))
                link(v.reciprocal(w1, w1))
                link(tt(w2, w1, st[:, 76:81], ALU.mult))
                v3 = w(W_V3, NT, 2, 3, E)
                for q, (hot, wk) in enumerate(((a1, w1), (a2, w2))):
                    a1c = C[:, C_A1:C_A1 + 2 * NT].rearrange("p (i k) -> p i k", k=2)[:, :, q]
                    for z, val in enumerate((a1c, C[:, C_T:C_T + NT], wk)):
                        link(tt(v3[:, :, q, z, :], hot, b3(val, E), ALU.mult))
                layer_wait(dve, l, "cnt_mm", 1)
                for q, hot in enumerate((a1, a2)):
                    link(tt(t1, hot, bank(6, NT, E), ALU.mult))
                    link(v.tensor_reduce(st[:, 24 + NT * q:24 + NT * q + NT], t1, AX, ALU.add))
                cnt, nbp = w(R_ME, E, rows=1), w(R_M2, E, rows=1)
                link(v.tensor_copy(cnt, ps[0:1, 6, E * NT:E * NT + E]))
                link(v.memset(nbp, 1.0))
                for b in range(1, NB):
                    link(stt(out=nbp, in0=cnt, scalar=float(CAP * b), in1=nbp, op0=ALU.is_gt, op1=ALU.add))
                if l == 0:
                    link(v.memset(tabf[:, :, :], 0.0))
                else:
                    link(v.tensor_copy(tabf[:, 0:1, :], tabf[:, PAIRS:PAIRS + 1, :]))
                tf = tabf[:, :, :].rearrange("o i (j k) -> o i j k", k=2)
                link(v.tensor_copy(tf[:, 0:PAIRS, :, 1], nbp.rearrange("o (i j) -> o i j", j=2)))
                for i in range(PAIRS):
                    link(tt(tf[:, i + 1, :, 0], tf[:, i, :, 0], tf[:, i, :, 1], ALU.add))
                v.tensor_copy(tab[l][:, :, :], tabf[:, :, :]).then_inc(L["bounds"], 1)
                layer_wait(dve, l, "slots_in", 16)
                for q in range(2 * NT):
                    i, k = divmod(q, 2)
                    if q >= 2:
                        layer_wait(dve, l, "list_mm", q - 1)
                    ts(w(W_OH, 2, NB * CAP)[:, q % 2, :], w(W_SLOT, NB * CAP), st[:, 24 + NT * k + i:25 + NT * k + i],
                       None, ALU.is_equal).then_inc(L["oh_ok"], 1)
                layer_wait(dve, l, "list_mm", 2 * NT)
                li = w(W_LI, NB, E, 2, rows=CAP).bitcast(I32)
                lw = w(W_LW, NB, E, rows=CAP)
                for b0, nb in ((0, 5), (5, NB - 5)):
                    pv = bank(b0 // 5, nb, 3, E, rows=CAP)
                    row = w(W_OH, nb, E, rows=CAP)
                    link(ts(row, pv[:, :, 0, :], 0.0, OOB, ALU.is_equal, ALU.mult))
                    link(stt(out=row, in0=pv[:, :, 0, :], scalar=-1.0, in1=row, op0=ALU.add, op1=ALU.add))
                    link(v.tensor_copy(li[:, b0:b0 + nb, :, 1], row))
                    link(v.tensor_copy(li[:, b0:b0 + nb, :, 0], pv[:, :, 1, :]))
                    link(v.tensor_copy(lw[:, b0:b0 + nb, :], pv[:, :, 2, :]))
                meet(dve, k0)

                def one_pass(j, n):
                    m = M[j]
                    dve.wait_ge(m["silu_ok"], n + 1)
                    dve.wait_ge(m["down_mm"], n)
                    tt(w(W_HH + 256 * j, 256), w(W_GT + 256 * j, 256), ps[:, 2 + j, 256:512], ALU.mult).then_inc(
                        m["h_ok"], 1)
                    dve.wait_ge(m["down_mm"], n + 1)
                    dve.wait_ge(m["scattered"], 16 * n)
                    ts(w(W_Y + D * j + 512, 512, rows=CAP), ps[0:CAP, 5 + 2 * j, :], wj[j][:, :], None,
                       ALU.mult).then_inc(m["yd_ok"], 1)

                every_pass(dve, l, one_pass)
                meet(dve, k0 + 1)
                repeat(mod(l, 5))
                layer_wait(dve, l, "gate2_ev", 4)
                for i in range(NT):
                    y = w(W_YB, 2, 2, D, rows=rows(i))[:, i % 2]
                    layer_wait(dve, l, f"y_in{i % 2}", 16 * (i // 2) + 16)
                    link(tt(y[:, 0, :], y[:, 0, :], y[:, 1, :], ALU.add))
                    tt(y[:, 0, :], y[:, 0, :], w(W_G if i < LS else W_GS, D, rows=rows(i)), ALU.mult).then_inc(
                        L["y_mul"], 1)

            ffn(0, 7)
            meet(dve, 9)
            norm(1)
            norm_ev(1)
            vp, y3 = w(W_VP, 2 + TP), w(W_Y3, T)
            link(v.memset(vp[:, 0:2], 0.0))
            dve.wait_ge(S["vs_tr"], 1)
            v.tensor_copy(vS[:, :, :, 0:2], bank(7, KD, NSEQ, 2)).then_inc(S["vs_ok"], 1)
            dve.wait_ge(S["vs_ok"], 1)
            y3s = y3[:, TP:T].rearrange("p (s t) -> p s t", t=TS)
            for c in range(KD):
                b = 4 * (c % 2)
                g = w(W_CG, 2, T)[:, c % 2, :]
                dve.wait_ge(S["cg_ok"], 2 * c + 2)
                link(tt(vp[:, 2:2 + TP], g[:, 0:TP], ps[:, b + 2, :], ALU.mult))
                link(tt(vS[:, c, :, 2:2 + TS], g[:, TP:T].rearrange("p (s t) -> p s t", t=TS),
                        bank(b + 3, NSEQ, TS, at=2 * NS), ALU.mult))
                link(v.tensor_copy(vK[:, c, :], vp[:, TP:TP + 2]))
                link(v.tensor_copy(vN[:, c, :].rearrange("p (s t) -> p s t", t=TS), vS[:, c, :, 2:2 + TS]))
                link(ts(y3[:, 0:TP], vp[:, 0:TP], ccw[:, 0, c:c + 1], None, ALU.mult))
                link(ts(y3s, vS[:, c, :, 0:TS], ccw[:, 0, c:c + 1], None, ALU.mult))
                for k in (1, 2):
                    link(stt(out=y3[:, 0:TP], in0=vp[:, k:k + TP], scalar=ccw[:, k, c:c + 1], in1=y3[:, 0:TP],
                             op0=ALU.mult, op1=ALU.add))
                    link(stt(out=y3s, in0=vS[:, c, :, k:k + TS], scalar=ccw[:, k, c:c + 1], in1=y3s,
                             op0=ALU.mult, op1=ALU.add))
                link(tt(zT[:, c, 0:TP], y3[:, 0:TP], ps[:, b, :], ALU.mult))
                tt(zT[:, c, TP:T], y3[:, TP:T], ps[:, b + 3, 0:NS], ALU.mult).then_inc(S["z_ok"], 1)
            meet(dve, 10)
            out_mul(1)
            meet(dve, 11)
            ffn(1, 12)

        @block.gpsimd
        def _(pool):
            g = nc.gpsimd
            meet(pool, 0)
            for u in range(2 * NT):
                i, r = u % NT, rows(u % NT)
                pool.wait_ge(S["tok_n"], u + 1)
                rv = raw[0:r, u % 3, :].rearrange("p (h d) -> p h d", h=H)
                g.tensor_tensor(rv, rv, qkg[0:r, u // NT:u // NT + 1, :].to_broadcast([r, H, P]), ALU.mult).then_inc(
                    S["tok_g"], 1)
                if u >= NT:
                    pool.wait_ge(S["tok_g"], u + 1)
                    if u > NT:
                        pool.wait_ge(S["kv_out"], 16 * (u - NT))
                    dst = (o["k_prompt"][0, 0, toks(i)].rearrange("t h d -> t (h d)") if i < LS
                           else o["k_sample"][0].rearrange("s t h d -> (s t) (h d)"))
                    pool.dma_start(dst, raw[0:r, u % 3, :]).then_inc(S["kv_out"], 16)
            for i in range(NT):
                pool.wait_ge(S["tok_copy"], 2 * NT + i + 1)
                dst = (o["v_prompt"][0, 0, toks(i)].rearrange("t h d -> t (h d)") if i < LS
                       else o["v_sample"][0].rearrange("s t h d -> (s t) (h d)"))
                pool.dma_start(dst, V[0:rows(i), i, :]).then_inc(S["kv_out"], 16)
            pool.wait_ge(S["kv_out"], 32 * NT)
            for k in range(1, 6):
                meet(pool, k)

            def out_add(l):
                for u in range(2 * NT):
                    z, i = divmod(u, NT)
                    layer_wait(pool, l, "wo_mul", u + 1)
                    xv = X[0:rows(i), i, 512 * z:512 * z + 512]
                    g.tensor_tensor(xv, xv, w(W_YB, 2, 512, rows=rows(i))[:, u % 2, :], ALU.add).then_inc(
                        L["wo_add"], 1)

            out_add(0)
            meet(pool, 6)

            def ffn(l, k0):
                layer_wait(pool, l, "bc_ev", 8)
                for i in range(NT):
                    layer_wait(pool, l, "h_mul", i + 1)
                    hv = Hb[0:rows(i), i, :]
                    g.tensor_tensor(hv, hv, w(W_BP if i < LS else W_BS, D, rows=rows(i)), ALU.add).then_inc(
                        L["h_ok"], 1)
                meet(pool, k0)
                li = w(W_LI, NB * E, 2, rows=CAP).bitcast(I32)
                lw = w(W_LW, NB * E, rows=CAP)

                def gather(j, n, col):
                    m = M[j]
                    pool.wait_ge(m["scattered"], 16 * n)
                    carry(pool)
                    g.tensor_copy(ix[j][:, :], li[:, bass.ds(col, 1), :].rearrange("p o k -> p (o k)")).then_inc(m["idx"], 1)
                    g.tensor_copy(wj[j][:, :], lw[:, bass.ds(col, 1)]).then_inc(m["idx"], 1)
                    pool.wait_ge(m["idx"], 2 * n + 2)
                    pool.wait_ge(m["xt_mm"], n)
                    carry(pool)
                    g.indirect_dma_start(out=w(W_XG + D * j, D, rows=CAP), out_offset=None, in_=h_dram,
                                         in_offset=bass.IndirectOffsetOnAxis(ap=ix[j][:, 0:1], axis=0),
                                         bounds_check=T - 1, oob_is_err=False).then_inc(m["gathered"], 16)

                def scatter(j, n):
                    m = M[j]
                    pool.wait_ge(m["ya_ok"], n + 1)
                    pool.wait_ge(m["yd_ok"], n + 1)
                    carry(pool)
                    g.indirect_dma_start(out=y_dram, out_offset=bass.IndirectOffsetOnAxis(ap=ix[j][:, 1:2], axis=0),
                                         in_=w(W_Y + D * j, D, rows=CAP), in_offset=None,
                                         bounds_check=2 * T - 1, oob_is_err=False).then_inc(m["scattered"], 16)

                def rest(j, v, e):
                    with pool.If(v[2 * j + 1] > 1):
                        with pool.Fori(1, NB) as b:
                            with pool.If(v[2 * j + 1] > b):
                                gather(j, v[2 * j] + b, b * E + e)
                                scatter(j, v[2 * j] + b)
                            pool.nop()
                        pool.nop()
                    pool.nop()

                gather(0, pool.value_load(tab[l][0:1, 0:1, 0:1], min_val=0, max_val=2 * E * NB), 0)
                with pool.Fori(0, PAIRS - 1) as i:
                    v = passes(pool, l, i)
                    gather(1, v[2], 2 * i + 1)
                    scatter(0, v[0])
                    rest(0, v, 2 * i)
                    gather(0, v[0] + v[1], 2 * i + 2)
                    scatter(1, v[2])
                    rest(1, v, 2 * i + 1)
                v = passes(pool, l, PAIRS - 1)
                gather(1, v[2], E - 1)
                scatter(0, v[0])
                rest(0, v, E - 2)
                scatter(1, v[2])
                rest(1, v, E - 1)
                for j in range(2):
                    n = pool.value_load(tab[l][0:1, PAIRS:PAIRS + 1, 2 * j:2 * j + 1], min_val=0, max_val=2 * E * NB)
                    pool.wait_ge(M[j]["scattered"], 16 * n)
                    carry(pool)
                meet(pool, k0 + 1)
                for i in range(NT):
                    layer_wait(pool, l, "y_mul", i + 1)
                    xv = X[0:rows(i), i, :]
                    g.tensor_tensor(xv, xv, w(W_YB, 2, 2, D, rows=rows(i))[:, i % 2, 0, :], ALU.add).then_inc(
                        L["y_add"], 1)

            ffn(0, 7)
            meet(pool, 9)
            meet(pool, 10)
            out_add(1)
            meet(pool, 11)
            ffn(1, 12)


_INS = ["x_prompt", "x_sample", "cache_k", "cache_v", "state_conv_b", "state_conv_c", "page_table", "c_prompt",
        "c_sample", "norm_mix_g", "norm_ffn_g", "w_ada", "b_ada", "w_in_a", "q_norm_g", "k_norm_g", "lam_q1", "lam_k1",
        "lam_q2", "lam_k2", "subln_g", "convb_w", "convb_b", "convb_ln_g", "convb_ln_b", "w_out_a", "w_in_c", "convc_w",
        "w_out_c", "w_group", "b_group", "w_router", "b_router", "w_gate_up", "w_down"]
_OUTS = [("y_prompt", (1, TP, D)), ("y_sample", (NSEQ, TS, D)), ("k_prompt", (1, 1, TP, H, P)),
         ("v_prompt", (1, 1, TP, H, P)), ("k_sample", (1, NSEQ, TS, H, P)), ("v_sample", (1, NSEQ, TS, H, P)),
         ("conv_b_prompt", (1, 1, PAD, 512)), ("conv_b_sample", (1, NSEQ, PAD, 512)),
         ("conv_c_prompt", (1, 1, 2, D)), ("conv_c_sample", (1, NSEQ, 2, D))]


def kernel(**inputs):
    import concourse.bacc as _bacc
    from concourse.bass_utils import run_bass_kernel_spmd as _run

    nc = _bacc.Bacc("TRN2", target_bir_lowering=False, num_devices=1)
    arrays, a = {}, {}
    given = {n: inputs[n] for n in _INS}
    given.update(consts=constants(), prompt_bias=prompt_bias(), sample_bias=sample_bias(), slot_numbers=slot_numbers())
    for name, x in given.items():
        x = np.ascontiguousarray(x)
        arrays[f"in_{name}_dram"] = x
        a[name] = nc.dram_tensor(f"in_{name}_dram", x.shape, mybir.dt.from_np(x.dtype), kind="ExternalInput").ap()
    o = {name: nc.dram_tensor(f"out_{name}_dram", shape, F32, kind="ExternalOutput").ap() for name, shape in _OUTS}
    hybrid_step(nc, a, o)
    r = _run(nc, [arrays], core_ids=[0])
    return tuple(r.results[0][f"out_{name}_dram"] for name, _ in _OUTS)
```

```python
from contextlib import ExitStack

import numpy as np

import concourse.bass as bass
from concourse import mybir

F32 = mybir.dt.float32
I32 = mybir.dt.int32
ALU = mybir.AluOpType
ACT = mybir.ActivationFunctionType
AX = mybir.AxisListType.X

P = 128
D = 1024
KD = D // P
TP, NSEQ, TS = 512, 8, 4
NS = NSEQ * TS
T = TP + NS
NT = TP // P + 1
LS = NT - 1
H, HD = 4, 64
PAST, PAGE = 1024, 128
NPG = PAST // PAGE
BW = 31
PAD = BW - 1
E, G, EG = 32, 4, 8
FE = 512
CAP = 128
NB = -(-T // CAP)
PAIRS = E // 2
OOB = 6000.0
BIG = 1e30
EPS = 1e-6
LAM_INIT = 0.2
NR = E + G
MODS = 6
SLOT = 4096
NSLOT = 6

C_ID, C_ONE, C_UP, C_I32, C_I32M, C_GRPM, C_VALID, C_A1, C_T, C_EPS, C_SEL, NC = (
    np.cumsum([0, P, P, P, E, E, E, NT, 2 * NT, NT, 1, 2 * 4 * H]).tolist())


def constants():
    c = np.zeros((P, NC), np.float32)
    p = np.arange(P)
    c[:, C_ID:C_ID + P] = np.eye(P)
    c[:, C_ONE:C_ONE + P] = 1
    c[:, C_UP:C_UP + P] = p[:, None] < p[None, :]
    c[:, C_I32:C_I32 + E] = np.arange(E)
    c[:, C_I32M:C_I32M + E] = np.arange(E) - 99
    c[:, C_GRPM:C_GRPM + E] = np.arange(E) // EG - 99
    tok = p[:, None] + P * np.arange(NT)
    c[:, C_VALID:C_VALID + NT] = tok < T
    c[:, C_A1:C_A1 + 2 * NT] = (2 * tok[:, :, None] + np.arange(2) + 1).reshape(P, -1)
    c[:, C_T:C_T + NT] = tok
    c[:, C_EPS] = EPS
    r = np.arange(8 * H)
    for m in range(2):
        c[r, C_SEL + 16 * m + 4 * (r // 8) + r % 4] = (r // 4 % 2) == m
    return c


def slot_numbers():
    return np.tile(np.arange(NB * CAP, dtype=np.float32), (P, 1))


def prompt_bias():
    p, j = np.arange(P)[:, None], np.arange(TP)[None, :]
    dist = p - j + (TP - P)
    return np.stack([np.where(dist >= 0, -2.0 ** (-2 * (h + 1)) * dist, -BIG) for h in range(H)], 1).reshape(
        P, H * TP).astype(np.float32)


def sample_bias():
    r = np.arange(8 * H)
    slope, t = -2.0 ** (-2.0 * (r // 8 + 1)), r % 4
    past = slope[:, None] * (PAST + t[:, None] - np.arange(PAST)[None, :])
    key = np.arange(NS)
    new = []
    for b in range(NSEQ):
        dist = t[:, None] - (key % TS)[None, :]
        new.append(np.where((key[None, :] // TS == b) & (dist >= 0), slope[:, None] * dist, -BIG))
    return np.concatenate([past] + new, 1).astype(np.float32)


W_PRM, W_C, W_LAM = 0, 512, 1536
W_U, W_US, W_CV, W_V, W_RAW, W_SG = 0, 2168, 3256, 5432, 7992, 9528
W_N = W_SG + T
W_PT, W_E = W_RAW, W_CV
W_QB, W_S, W_PS, W_KT, W_QC, W_QN = 2168, 3256, 4312, 7992, 9016, 9144
W_SQ, W_RN = W_CV, W_V
W_VP, W_CG, W_Y3, W_VS, W_VK, W_VN, W_ST, W_SO = 0, 514, 1602, 2146, 2530, 2546, 3072, 4096
W_AP, W_BP, W_AS, W_BS = 0, 1024, 2048, 3072
R_LG, R_ME, R_A1, R_A2, R_CC, R_T, R_M2 = 4096, 4280, 4440, 4600, 4760, 4920, 5080
W_OH, W_V3, W_LI, W_LW, W_SLOT = 5300, 6600, 8312, 8640, 9060
W_XG, W_XT, W_HH, W_HT, W_Y = 0, 2048, 4096, 5120, 6144
W_ROW = 2048
W_YB, W_G, W_GS = 2048, 6200, 7224
W_RA, W_RB = 9760, 5300
W_SLOT_END = W_SLOT + NB * CAP
assert W_SLOT_END <= W_RA and W_RA + KD * NS <= W_N and W_V3 + 960 <= W_LI and W_Y + 2 * D <= W_LI


def hybrid_step(nc, a, o):
    with ExitStack() as ctx:
        def sb(name, shape, dt=F32):
            return ctx.enter_context(nc.sbuf_tensor(name, shape, dt))

        def sem(name):
            return ctx.enter_context(nc.semaphore(name))

        ring = sb("ring", [P, NSLOT, SLOT])
        X = sb("X", [P, NT, D])
        Hb = sb("Hb", [P, NT, D])
        hT = sb("hT", [P, KD, T])
        W = sb("W", [P, W_N])
        C = sb("C", [P, NC])
        modT = sb("modT", [P, 2 * MODS * KD, 9])
        scT = sb("scT", [P, 4, KD, 9])
        wr = sb("wr", [P, 2, KD, NR])
        rb = sb("rb", [P, 2, NR])
        prm = sb("prm", [P, 289])
        qkg = sb("qkg", [P, 2, P])
        lamw = sb("lamw", [P, 8])
        cT = sb("cT", [P, KD, 9])
        st = sb("st", [P, 96])
        cmb = sb("cmb", [8 * H, 32])
        pgt = sb("pgt", [1, NSEQ * NPG], I32)
        tabf = sb("tabf", [1, 4, E + 1])
        tab = [sb(f"tab{l}", [1, 2, E], I32) for l in range(2)]
        gix = [sb(f"gix{j}", [CAP, 1], I32) for j in range(3)]
        six = [sb(f"six{j}", [CAP, 1], I32) for j in range(3)]
        wj = [sb(f"wj{j}", [CAP, 1]) for j in range(3)]
        ps = ctx.enter_context(nc.psum_tensor("ps", [P, 8, 512], F32))
        h_dram = nc.dram_tensor("h_rows", (T, D), F32).ap()
        y_dram = nc.dram_tensor("y_rows", (2 * T, D), F32).ap()

        ident, ones, upper = C[:, C_ID:C_ID + P], C[:, C_ONE:C_ONE + P], C[:, C_UP:C_UP + P]
        epsc = C[:, C_EPS:C_EPS + 1]
        bT = prm[:, 0:96]
        gT = prm[:, 96:128].rearrange("p (n c) -> p n c", c=KD)
        cbb, lng, lnb, subg = prm[:, 128:132], prm[:, 132:136], prm[:, 136:140], prm[:, 140:141]
        ccw = prm[:, 141:165].rearrange("p (w c) -> p w c", c=KD)
        cbw = prm[:, 165:289].rearrange("p (w c) -> p w c", c=4)
        neglam = lamw[:, 4:5]

        def w(at, *dims, rows=P):
            v = W[0:rows, at:at + int(np.prod(dims))]
            if len(dims) == 1:
                return v
            n = "abcd"[:len(dims)]
            return v.rearrange(f"p ({' '.join(n)}) -> p {' '.join(n)}", **dict(zip(n, dims)))

        def bank(b, *dims, rows=P, at=0):
            v = ps[0:rows, b, at:at + int(np.prod(dims))]
            if len(dims) == 1:
                return v
            n = "abcd"[:len(dims)]
            return v.rearrange(f"p ({' '.join(n)}) -> p {' '.join(n)}", **dict(zip(n, dims)))

        uT, uS = w(W_U, 4, PAD + TP), w(W_US, 4, NSEQ, PAD + TS)
        cv, V, raw, sg = w(W_CV, 4, T), w(W_V, NT, 512), w(W_RAW, 3, 512), w(W_SG, T)
        hflat = Hb[:, :, :].rearrange("p a b -> p (a b)")
        QT = hflat[:, 0:H * T].rearrange("p (h t) -> p h t", h=H)
        KT = hflat[:, H * T:2 * H * T].rearrange("p (h t) -> p h t", h=H)
        sq = hflat[:, 2 * H * T:2 * H * T + 512]
        zT = hflat[:, 0:KD * T].rearrange("p (c t) -> p c t", c=KD)
        vS, vK, vN = w(W_VS, KD, NSEQ, 2 + TS), w(W_VK, KD, 2), w(W_VN, KD, NS)

        def lane(what, j):
            at, dims = {"xg": (0, (KD, P)), "xt": (1, (KD, CAP)), "hh": (2, (FE,)), "ht": (2.5, (FE // P, CAP)),
                        "y": (3, (D,))}[what]
            n = int(np.prod(dims))
            v = w({"xg": W_XG, "xt": W_XT, "hh": W_HH, "ht": W_HT, "y": W_Y}[what] + n * j, n) if j < 2 else (
                hflat[:, int(at * D):int(at * D) + n])
            return v if len(dims) == 1 else v.rearrange("p (a b) -> p a b", a=dims[0])

        def rows(i):
            return P if i < LS else NS

        def toks(i):
            return slice(P * i, P * i + rows(i))

        def mod(l, m):
            return modT[:, MODS * KD * l + KD * m:MODS * KD * l + KD * m + KD, :]

        slot_in = [sem(f"slot_in{s}") for s in range(NSLOT)]
        slot_free = [sem(f"slot_free{s}") for s in range(NSLOT)]
        phase_end = sem("phase_end")
        S = {n: sem(n) for n in (
            "params_in x_in page_in stats_set c_silu c_tr c_ev row_ok row_tr prm_tr prm_ev lam_sum lam_exp ada_ev "
            "u_mm u_sig u_ok u_state st_tr st_ev conv un_ok uo_tr uo_ev "
            "tok_mm tok_copy tok_sq tok_ss tok_root tok_n tok_g tok_tr tok_ev kv_out "
            "bias_in at_s at_b at_m at_e at_p at_tr at_pt at_o at_ov "
            "qb_ok sp_q sp_kt sp_eva sp_evd sp_s sp_d sp_e sp_pt sp_ptev sp_ov "
            "on_sq on_mm on_root on_ok ln_mm ln_x ln_sq ln_root ln_n out_dma "
            "bch_mm cg_ok z_ok vs_in vs_tr vs_ok vo_tr vo_ok dve carried").split()}
        per_layer = dict(rms1_sum=NT, rms1_root=1, rms1_inv=1, rms2_sum=NT, rms2_root=1, xn_a=2, xn_d=3, tr1=KD + 1,
                         ev1a=4, ev1d=5, gate_mm=1, gate_ev=4, wo_mm=2 * NT, wo_mul=2 * NT, wo_add=2 * NT, bc_mm=1,
                         bc_ev=8, rep_ok=4, h_mul=NT, h_ok=NT, h_out=16 * NT, slots_in=16, tr2=KD + 1, ev2a=4, ev2d=5, lg_mm=1,
                         r_dif=1, r_exp=1, r_ok=1, cnt_mm=1, oh_ok=2 * NT, list_mm=2 * NT, bounds=1, gate2_mm=1,
                         gate2_ev=4, y_in0=48, y_in1=32, y_mul=NT, y_add=NT)
        L = {n: sem(n) for n in per_layer}

        def layer_wait(eng, l, name, n):
            eng.wait_ge(L[name], per_layer[name] * l + n)

        M = {n: sem("m_" + n) for n in "xt_mm xa_ok xd_ok gu_mm silu_ok h_ok ht_mm ht_ok down_mm ya_ok yd_ok".split()}
        gathered, scattered, listed = ([sem(f"{n}{j}") for j in range(2)] for n in ("gathered", "scattered", "listed"))
        gix_ok = [sem(f"gix_ok{j}") for j in range(2)]
        F = {n: sem("f_" + n) for n in "listed gathered products act dve scattered".split()}
        AHEAD = 2

        seq = 16 * NPG
        in0 = [80 + 4 * seq] * 4 + [96, 80]
        in1 = [in0[s] + 16 * PAIRS + (32 if s < 2 else 16) for s in range(NSLOT)]
        base_in = [in0, in1]

        def linker(eng, name):
            n = [0]

            def link(ins):
                n[0] += 1
                ins.then_inc(S[name], 1)
                eng.wait_ge(S[name], n[0])
            return link

        def meet(eng, k):
            eng.drain().then_inc(phase_end, 1)
            eng.wait_ge(phase_end, 4 * (k + 1))

        def done(l, n):
            return n + (E * l + AHEAD + 1)

        def lane_done(l, p, unit):
            return p * unit + (PAIRS * l + 1) * unit

        def lane_wait(eng, sems, j, l, p, unit):
            if not (isinstance(p, int) and lane_done(l, p, unit) == 0):
                eng.wait_ge(sems[j], lane_done(l, p, unit))

        def further(eng, l, e, one_pass):
            passes = eng.value_load(tab[l][0:1, 0, bass.ds(e, 1)], min_val=1, max_val=NB)
            with eng.If(passes > 1):
                before = eng.value_load(tab[l][0:1, 1, bass.ds(e, 1)], min_val=0, max_val=2 * T)
                with eng.Fori(1, NB) as b:
                    with eng.If(passes > b):
                        one_pass(before + b, b)
                    eng.nop()
                eng.nop()
            eng.nop()

        def each_expert(eng, l, step):
            step(0, 0, 0, first=True)
            step(1, 1, 0)
            step(2, 0, 1)
            with eng.Fori(1, PAIRS - 1) as i:
                step(2 * i + 1, 1, i)
                step(2 * i + 2, 0, i + 1)
            step(E - 1, 1, PAIRS - 1, last=True)

        def carry(eng):
            eng.sem_inc(S["carried"], 1)

        block = ctx.enter_context(nc.Block())

        @block.sync
        def _(sp):
            def load(s, src):
                sp.dma_start(ring[:, s, :].rearrange("p (k n) -> p k n", k=KD), src).then_inc(slot_in[s], 16)

            ada = a["w_ada"].rearrange("l (k p) n -> l p k n", p=P)
            with sp.Fori(0, 2) as l:
                with sp.Fori(0, 2) as h:
                    for s in range(NSLOT):
                        sp.wait_ge(slot_free[s], 2 * l + h + 1)
                        load(s, ada[l, :, :, bass.ds(h * (3 * D) + 512 * s, 512)])
            wina = a["w_in_a"][0].rearrange("(k p) n -> p k n", p=P)
            for s, col in enumerate((3, 4, 0, 1, 2)):
                sp.wait_ge(slot_free[s], 5)
                load(s, wina[:, :, 512 * col:512 * col + 512])
            wouta = a["w_out_a"][0].rearrange("(k p) n -> p k n", p=P)
            sp.wait_ge(slot_free[5], 5)
            load(5, wouta[:, :, 0:512])
            sp.wait_ge(S["page_in"], 16)
            ck = a["cache_k"][0].rearrange("n r h d -> n r (h d)")
            cvd = a["cache_v"][0].rearrange("n r h d -> n r (h d)")
            sp.wait_ge(S["u_mm"], 4)
            sp.wait_ge(S["tok_mm"], 2 * NT)
            with sp.Fori(0, 4) as it:
                for s in range(4):
                    sp.wait_ge(S["page_in"], 16)
                    sp.wait_ge(slot_free[s], it + 5)
                    for g in range(NPG):
                        page = sp.value_load(pgt[0:1, bass.ds(it * (2 * NPG) + (s // 2) * NPG + g, 1)],
                                             min_val=0, max_val=a["cache_k"].shape[1] - 1)
                        sp.dma_start(ring[:, s, 512 * g:512 * g + 512],
                                     (ck if s % 2 == 0 else cvd)[page, :, :]).then_inc(slot_in[s], 16)
            sp.wait_ge(S["tok_mm"], 3 * NT)
            load(4, wouta[:, :, 512:1024])

            def experts(l):
                gu = a["w_gate_up"][l].rearrange("e (k p) n -> e p k n", p=P)
                dn = a["w_down"][l].rearrange("e (k p) n -> e p k n", p=P)

                def part(e, j, k):
                    src = gu[e, :, 4 * k:4 * k + 4, :] if k < 2 else dn[e, :, :, :]
                    sp.dma_start(ring[:, 3 * j + k, :].rearrange("p (k n) -> p k n", k=4), src).then_inc(
                        slot_in[3 * j + k], 16)

                for s in range(NSLOT):
                    if l == 0 and s < 4:
                        sp.wait_ge(slot_free[s], 9)
                    elif l == 0:
                        layer_wait(sp, 0, "wo_mm", NT if s == 5 else 2 * NT)
                    elif s < 2:
                        layer_wait(sp, 1, "wo_mm", NT * (s + 1))
                    else:
                        sp.wait_ge(S["bch_mm"], 4 * (s // 3 + 1))
                    part(s // 3, s // 3, s % 3)
                def step(n, j, p):
                    sp.wait_ge(M["ht_mm"], done(l, n - 2))
                    part(n, j, 0)
                    part(n, j, 1)
                    sp.wait_ge(M["down_mm"], done(l, n - 2))
                    part(n, j, 2)

                with sp.Fori(1, PAIRS) as i:
                    step(2 * i, 0, i)
                    step(2 * i + 1, 1, i)
                sp.wait_ge(M["down_mm"], done(l, E - 1))

            experts(0)
            winc = a["w_in_c"][0].rearrange("(k p) n -> p k n", p=P)
            for s in range(NSLOT):
                col = D * (s % 3) + 512 * (s // 3)
                load(s, winc[:, :, col:col + 512])
            woutc = a["w_out_c"][0].rearrange("(k p) n -> p k n", p=P)
            sp.wait_ge(S["bch_mm"], 4)
            for s in range(2):
                load(s, woutc[:, :, 512 * s:512 * s + 512])
            experts(1)

        @block.tensor
        def _(pe):
            mm, tr = nc.tensor.matmul, nc.tensor.transpose

            def tile8(s):
                return ring[:, s, :].rearrange("p (k n) -> p k n", k=KD)

            for n in ("xt_mm", "gu_mm", "ht_mm", "down_mm"):
                pe.sem_inc(M[n], AHEAD)
            pe.wait_ge(S["params_in"], 16 * 26)
            tr(ps[:, 6, 0:96], W[0:96, 0:P], ident[0:96, 0:96])
            tr(ps[:, 6, 96:165], W[0:69, P:2 * P], ident[0:69, 0:69])
            tr(ps[:, 6, 165:289], W[0:124, 2 * P:3 * P], ident[0:124, 0:124]).then_inc(S["prm_tr"], 1)
            pe.wait_ge(S["c_silu"], 1)
            for c in range(KD):
                x = tr(ps[:, 7, 9 * c:9 * c + 9], W[0:9, W_C + P * c:W_C + P * c + P], ident[0:9, 0:9])
            x.then_inc(S["c_tr"], 1)
            pe.wait_ge(S["c_ev"], 1)
            def row_turns(it, s):
                n = NSLOT * it + s
                pe.wait_ge(S["row_ok"], n + 1)
                pe.wait_ge(S["ada_ev"], n + 1)
                carry(pe)
                for m in range(4):
                    x = tr(ps[:, 2 + s % 2, 9 * m:9 * m + 9], w(W_ROW, 2, 4, P, rows=9)[:, s % 2, m, :], ident[0:9, 0:9])
                x.then_inc(S["row_tr"], 1)

            pe.sem_inc(S["row_tr"], 2)
            for s in range(NSLOT):
                pe.sem_inc(slot_free[s], 1)
            with pe.Fori(0, 4) as it:
                for s in range(NSLOT):
                    pe.wait_ge(slot_in[s], 16 * it + 16)
                    if s >= 2:
                        pe.wait_ge(S["row_ok"], NSLOT * it + (s - 1))
                    for k in range(KD):
                        x = mm(ps[0:9, s % 2, :], cT[:, k, :], tile8(s)[:, k, :], start=(k == 0), stop=(k == KD - 1))
                    x.then_inc(slot_free[s], 1)
                    if s >= 1:
                        row_turns(it, s - 1)
                row_turns(it, NSLOT - 1)
            meet(pe, 0)

            def norm_transposes(l):
                layer_wait(pe, l, "xn_a", 2)
                layer_wait(pe, l, "xn_d", 3)
                for c in range(KD):
                    if c >= 4:
                        layer_wait(pe, l, "ev1a" if c % 2 == 0 else "ev1d", (c - 4) // 2 + 1)
                    for i in range(4):
                        x = tr(ps[:, c % 4, P * i:P * i + P], Hb[:, i, P * c:P * c + P], ident)
                    x.then_inc(L["tr1"], 1)
                for c in range(KD):
                    x = tr(ps[:, 4, NS * c:NS * c + NS], Hb[0:NS, LS, P * c:P * c + P], ident[0:NS, 0:NS])
                x.then_inc(L["tr1"], 1)
                layer_wait(pe, l, "ev1a", 4)
                layer_wait(pe, l, "ev1d", 5)

            def spread(l, n, src, b0, at=W_RA):
                for c in range(KD):
                    mm(ps[:, b0 + c // 4, P * (c % 4):P * (c % 4) + P], src[:, c, 0:1].to_broadcast([P, P]), ident,
                       start=True, stop=True)
                layer_wait(pe, l, "rep_ok", n)
                for c in range(KD):
                    x = mm(ps[0:NS, b0 + 2 + c // 4, P * (c % 4):P * (c % 4) + P], w(at, KD, NS)[:, c, :], ident,
                           start=True, stop=True)
                return x

            def out_proj(l, yT, slots, arrived):
                for n, s in enumerate(slots):
                    pe.wait_ge(slot_in[s], arrived[n])
                    for i in range(NT):
                        u = n * NT + i
                        if u >= 4:
                            layer_wait(pe, l, "wo_mul", u - 3)
                        for k in range(KD):
                            x = mm(ps[0:rows(i), u % 4, :], yT[:, k, toks(i)], tile8(s)[:, k, :],
                                   start=(k == 0), stop=(k == KD - 1))
                        x.then_inc(L["wo_mm"], 1)

            norm_transposes(0)
            pe.wait_ge(slot_in[0], 80)
            pe.wait_ge(slot_in[1], 80)
            for m in range(4):
                if m >= 2:
                    pe.wait_ge(S["u_ok"], 2 * (m - 1))
                for s in range(2):
                    ws = tile8(s)[:, :, P * m:P * m + P]
                    for k in range(KD):
                        mm(ps[:, 2 * (m % 2) + s, :], ws[:, k, :], hT[:, k, 0:TP], start=(k == 0), stop=(k == KD - 1))
                    for k in range(KD):
                        x = mm(ps[:, 4 + m % 2, NS * s:NS * s + NS], ws[:, k, :], hT[:, k, TP:T],
                               start=(k == 0), stop=(k == KD - 1))
                x.then_inc(S["u_mm"], 1)
            pe.wait_ge(S["u_state"], 32)
            for r in range(2):
                for c in range(4):
                    x = tr(ps[:, 6 + r, 120 * c:120 * c + 120], w(W_CV + 512 * r, 4, P, rows=120)[:, c, :],
                           ident[0:120, 0:120])
            x.then_inc(S["st_tr"], 1)
            pe.wait_ge(S["st_ev"], 2)
            pe.wait_ge(S["u_ok"], 8)
            for u in range(3 * NT):
                s, i = 2 + u // NT, u % NT
                if i == 0:
                    pe.wait_ge(slot_in[s], 80)
                if u >= 4:
                    pe.wait_ge(S["tok_copy"], u - 3)
                for k in range(KD):
                    x = mm(ps[0:rows(i), u % 4, :], hT[:, k, toks(i)], tile8(s)[:, k, :],
                           start=(k == 0), stop=(k == KD - 1))
                x.then_inc(S["tok_mm"], 1)
                v = u - 1
                if 0 <= v < 2 * NT:
                    r = rows(v % NT)
                    pe.wait_ge(S["tok_g"], v + 1)
                    if v >= 2:
                        pe.wait_ge(S["tok_ev"], v - 1)
                    for c in range(H):
                        x = tr(ps[:, 6 + v % 2, P * c:P * c + r], raw[0:r, v % 3, P * c:P * c + P], ident[0:r, 0:r])
                    x.then_inc(S["tok_tr"], 1)
            meet(pe, 1)
            for c in range(4):
                mm(ps[:, 0, :], ones, cv[:, c, 0:TP], start=(c == 0), stop=(c == 3))
            for c in range(4):
                x = mm(ps[:, 1, 0:NS], ones, cv[:, c, TP:T], start=(c == 0), stop=(c == 3))
            x.then_inc(S["ln_mm"], 1)
            pe.wait_ge(S["un_ok"], 1)
            for c in range(4):
                tr(ps[0:PAD, 6, P * c:P * c + P], uT[:, c, TP:TP + PAD], ident)
            for c in range(4):
                x = tr(ps[0:NS, 7, P * c:P * c + P], w(W_SG, 4, NS)[:, c, :], ident)
            x.then_inc(S["uo_tr"], 1)
            for c in range(4):
                pe.wait_ge(S["ln_sq"], c + 1)
                v = w(W_RAW, 2, T)[:, c % 2, :]
                mm(ps[:, 2, :], ones, v[:, 0:TP], start=(c == 0), stop=(c == 3), skip_group_check=True)
                x = mm(ps[:, 3, 0:NS], ones, v[:, TP:T], start=(c == 0), stop=(c == 3), skip_group_check=True)
                x.then_inc(S["ln_mm"], 1)
            meet(pe, 2)

            def scores(u):
                h, i = divmod(u, 4)
                if u >= 2:
                    pe.wait_ge(S["at_b"], 2 * (u - 1))
                for m in range(2):
                    x = mm(ps[:, 2 * (u % 2) + m, 0:P * (i + 1)], QT[HD * m:HD * m + HD, h, P * i:P * i + P],
                           KT[HD * m:HD * m + HD, h, 0:P * (i + 1)], start=True, stop=True)
                x.then_inc(S["at_s"], 1)

            scores(0)
            for u in range(4 * H):
                h, i = divmod(u, 4)
                if u + 1 < 4 * H:
                    scores(u + 1)
                pe.wait_ge(S["at_p"], u + 1)
                if u >= 2:
                    pe.wait_ge(S["at_pt"], u - 1)
                for c in range(i + 1):
                    x = tr(ps[:, 4 + u % 2, P * c:P * c + P], w(W_E, 4, 4, P)[:, 2 * (u % 2), c, :], ident)
                x.then_inc(S["at_tr"], 1)
                if i == 3:
                    pe.wait_ge(S["at_pt"], u + 1)
                    if h >= 2:
                        pe.wait_ge(S["at_ov"], h - 1)
                    for c in range(4):
                        x = mm(ps[:, 6 + h % 2, P * c:TP], V[:, c, P * h:P * h + P], w(W_PT, 4, TP)[:, c, P * c:TP],
                               start=(c == 0), stop=(c == 3), skip_group_check=True)
                    x.then_inc(S["at_o"], 1)
            meet(pe, 3)
            pe.sem_inc(S["sp_s"], 1)
            pe.sem_inc(S["sp_pt"], 1)

            def key_turns(sk, q):
                for g in range(4):
                    at = 512 * (4 * (q // 4) + g) + P * (q % 4)
                    x = tr(ps[:, 3 + q % 2, P * g:P * g + P], ring[:, sk, at:at + P], ident)
                x.then_inc(S["sp_kt"], 1)

            with pe.Fori(0, 4) as it:
                for b in range(2):
                    sk, sv, n = 2 * b, 2 * b + 1, 2 * it + b
                    pe.wait_ge(slot_in[sk], seq * it + (seq + 80))
                    key_turns(sk, 0)
                    pe.wait_ge(S["sp_q"], n + 1)
                    pe.wait_ge(S["sp_d"], 8 * n + 8)
                    for q in range(2 * H):
                        if q < 2 * H - 1:
                            key_turns(sk, q + 1)
                        pe.wait_ge(S["sp_eva" if q % 2 == 0 else "sp_evd"], 4 * n + (q // 2 + 1))
                        mm(ps[0:32, q // 4, :], w(W_QC, H, 32)[:, q % 4, :], w(W_KT, 2, 512)[:, q % 2, :],
                           start=(q % 4 == 0), stop=(q % 4 == H - 1), skip_group_check=True).then_inc(S["sp_s"], 1)
                    for h in range(H):
                        x = mm(ps[0:32, 2, 0:NS], w(W_QC, H, 32)[:, h, :], KT[:, h, TP:T],
                               start=(h == 0), stop=(h == H - 1))
                    x.then_inc(slot_free[sk], 1)
                    pe.wait_ge(S["sp_d"], 8 * n + 16)
                    for g in range(NPG + 1):
                        k = P if g < NPG else NS
                        x = mm(ps[0:k, 5, 16 * g:16 * g + 16], w(W_S, PAST + NS, rows=32)[:, P * g:P * g + k],
                               cmb[:, 16:32], start=True, stop=True)
                    x.then_inc(S["sp_pt"], 1)
                    pe.wait_ge(slot_in[sv], seq * it + (seq + 80))
                    pe.wait_ge(S["sp_ptev"], 2 * n + 2)
                    pe.wait_ge(S["sp_ov"], n + 1)
                    pT = w(W_PS, NPG + 1, 16)
                    for h in range(H):
                        for g in range(NPG):
                            mm(ps[:, 6, TS * h:TS * h + TS], ring[:, sv, 512 * g + P * h:512 * g + P * h + P],
                               pT[:, g, TS * h:TS * h + TS], start=(g == 0), stop=False)
                        x = mm(ps[:, 6, TS * h:TS * h + TS], V[0:NS, LS, P * h:P * h + P],
                               pT[0:NS, NPG, TS * h:TS * h + TS], start=False, stop=True)
                    x.then_inc(slot_free[sv], 1)
            meet(pe, 4)
            for h in range(H):
                pe.wait_ge(S["on_sq"], h + 1)
                v = w(W_SQ, 2, T)[:, h % 2, :]
                mm(ps[:, h, :], ones, v[:, 0:TP], start=True, stop=True)
                mm(ps[:, 4, NS * h:NS * h + NS], ones, v[:, TP:T], start=True, stop=True).then_inc(S["on_mm"], 1)
            meet(pe, 5)
            spread(0, 1, mod(0, 2), 4).then_inc(L["gate_mm"], 1)
            out_proj(0, hT, (5, 4), (80, 96))
            meet(pe, 6)

            def ffn(l, k0):
                spread(l, 2, scT[:, 2 + l, :, :], 0)
                spread(l, 3, mod(l, 3), 4, W_RB).then_inc(L["bc_mm"], 1)
                layer_wait(pe, l, "bc_ev", 8)
                layer_wait(pe, l, "h_ok", NT)
                for c in range(KD):
                    if c >= 4:
                        layer_wait(pe, l, "ev2a" if c % 2 == 0 else "ev2d", (c - 4) // 2 + 1)
                    for i in range(4):
                        x = tr(ps[:, c % 4, P * i:P * i + P], Hb[:, i, P * c:P * c + P], ident)
                    x.then_inc(L["tr2"], 1)
                for c in range(KD):
                    x = tr(ps[:, 4, NS * c:NS * c + NS], Hb[0:NS, LS, P * c:P * c + P], ident[0:NS, 0:NS])
                x.then_inc(L["tr2"], 1)
                layer_wait(pe, l, "ev2a", 4)
                layer_wait(pe, l, "ev2d", 5)
                for i in range(NT):
                    for k in range(KD):
                        x = mm(ps[0:rows(i), 5, NR * i:NR * i + NR], hT[:, k, toks(i)], wr[:, l, k, :],
                               start=(k == 0), stop=(k == KD - 1))
                x.then_inc(L["lg_mm"], 1)
                layer_wait(pe, l, "r_ok", 1)
                cc = w(R_CC, NT, E)
                for i in range(NT):
                    for q in range(i + 1):
                        x = mm(ps[:, 6, E * i:E * i + E], upper if q == i else ones, cc[:, q, :],
                               start=(q == 0), stop=(q == i))
                for q in range(NT):
                    x = mm(ps[:, 6, E * NT:E * NT + E], ones, cc[:, q, :], start=(q == 0), stop=(q == NT - 1))
                x.then_inc(L["cnt_mm"], 1)
                for q in range(2 * NT):
                    layer_wait(pe, l, "oh_ok", q + 1)
                    for b in range(NB):
                        x = mm(ps[:, 0, 96 * b:96 * b + 96],
                               w(W_OH, 2, NB * CAP)[:, q % 2, CAP * b:CAP * b + CAP], w(W_V3, 2 * NT, 96)[:, q, :],
                               start=(q == 0 and b == 0), stop=(q == 2 * NT - 1), skip_group_check=True)
                    x.then_inc(L["list_mm"], 1)
                meet(pe, k0)

                def x_turns(xg, signal):
                    for k in range(KD):
                        x = tr(ps[:, k // 4, P * (k % 4):P * (k % 4) + P], xg[:, k, :], ident)
                    x.then_inc(signal, 1)

                def gate_up(xt, j, signal):
                    for k in range(KD):
                        for z in range(2):
                            at = D * (k % 4) + FE * z
                            x = mm(ps[:, 2 + z, :], xt[:, k, :], ring[:, 3 * j + k // 4, at:at + FE], start=(k == 0),
                                   stop=(k == KD - 1))
                    x.then_inc(signal, 1)

                def h_turns(hh, signal):
                    for k in range(FE // P):
                        x = tr(ps[:, 4, P * k:P * k + P], hh[:, P * k:P * k + P], ident)
                    x.then_inc(signal, 1)

                def down(ht, j, signal):
                    for k in range(FE // P):
                        for z in range(2):
                            at = D * k + 512 * z
                            x = mm(ps[:, 5 + z, :], ht[:, k, :], ring[:, 3 * j + 2, at:at + 512], start=(k == 0),
                                   stop=(k == FE // P - 1))
                    x.then_inc(signal, 1)

                def gathered_turns(n, j, p):
                    pe.wait_ge(gathered[j], lane_done(l, p, 16))
                    pe.wait_ge(M["xa_ok"], done(l, n - 1))
                    pe.wait_ge(M["xd_ok"], done(l, n - 1))
                    x_turns(lane("xg", j), M["xt_mm"])

                def last_product(n, j, p):
                    pe.wait_ge(M["ht_ok"], done(l, n))
                    pe.wait_ge(slot_in[3 * j + 2], p * 16 + (base_in[l][3 * j + 2] + 16))
                    pe.wait_ge(M["ya_ok"], done(l, n - 1))
                    pe.wait_ge(M["yd_ok"], done(l, n - 1))
                    down(lane("ht", j), j, M["down_mm"])

                def step(n, j, p, first=False, last=False):
                    pe.wait_ge(slot_in[3 * j], p * 16 + (base_in[l][3 * j] + 16))
                    pe.wait_ge(slot_in[3 * j + 1], p * 16 + (base_in[l][3 * j + 1] + 16))
                    pe.wait_ge(M["xa_ok"], done(l, n))
                    pe.wait_ge(M["xd_ok"], done(l, n))
                    pe.wait_ge(M["h_ok"], done(l, n - 1))
                    gate_up(lane("xt", j), j, M["gu_mm"])
                    if not last:
                        gathered_turns(n + 1, 1 - j, p + j)

                    def one_pass(c, b):
                        pe.wait_ge(F["gathered"], c * 16)
                        pe.wait_ge(M["xa_ok"], done(l, n if last else n + 1))
                        pe.wait_ge(M["xd_ok"], done(l, n if last else n + 1))
                        x_turns(lane("xg", 2), F["products"])
                        pe.wait_ge(F["act"], c * 4 - 3)
                        pe.wait_ge(F["dve"], c * 3 - 2)
                        pe.wait_ge(M["h_ok"], done(l, n))
                        gate_up(lane("xt", 2), j, F["products"])
                        pe.wait_ge(F["dve"], c * 3 - 1)
                        pe.wait_ge(M["ht_ok"], done(l, n - 1))
                        h_turns(lane("hh", 2), F["products"])
                        pe.wait_ge(F["act"], c * 4 - 1)
                        pe.wait_ge(slot_in[3 * j + 2], p * 16 + (base_in[l][3 * j + 2] + 16))
                        pe.wait_ge(M["ya_ok"], done(l, n - 2))
                        pe.wait_ge(M["yd_ok"], done(l, n - 2))
                        down(lane("ht", 2), j, F["products"])
                        pe.wait_ge(F["act"], c * 4)
                        pe.wait_ge(F["dve"], c * 3)

                    further(pe, l, n, one_pass)
                    if not first:
                        last_product(n - 1, 1 - j, p - 1 + j)
                    pe.wait_ge(M["h_ok"], done(l, n))
                    pe.wait_ge(M["ht_ok"], done(l, n - 1))
                    h_turns(lane("hh", j), M["ht_mm"])

                gathered_turns(0, 0, 0)
                each_expert(pe, l, step)
                last_product(E - 1, 1, PAIRS - 1)
                meet(pe, k0 + 1)
                spread(l, 4, mod(l, 5), 4).then_inc(L["gate2_mm"], 1)

            ffn(0, 7)
            meet(pe, 9)
            norm_transposes(1)
            pe.wait_ge(S["vs_in"], 16)
            for c in range(KD):
                x = tr(ps[:, 7, 16 * c:16 * c + 16], w(W_ST, D, rows=16)[:, P * c:P * c + P], ident[0:16, 0:16])
            x.then_inc(S["vs_tr"], 1)
            pe.wait_ge(S["vs_ok"], 1)
            for c in range(KD):
                if c >= 2:
                    pe.wait_ge(S["z_ok"], c - 1)
                for s in range(3):
                    r = 3 * (c // 4) + s
                    if c % 4 == 0:
                        pe.wait_ge(slot_in[r], in0[r] + 16 * PAIRS + 16)
                    ws = tile8(r)[:, :, P * (c % 4):P * (c % 4) + P]
                    for k in range(KD):
                        mm(ps[:, 4 * (c % 2) + s, :], ws[:, k, :], hT[:, k, 0:TP], start=(k == 0), stop=(k == KD - 1))
                    for k in range(KD):
                        x = mm(ps[:, 4 * (c % 2) + 3, NS * s:NS * s + NS], ws[:, k, :], hT[:, k, TP:T],
                               start=(k == 0), stop=(k == KD - 1))
                x.then_inc(S["bch_mm"], 1)
            meet(pe, 10)
            for c in range(KD):
                tr(ps[0:2, c // 4, P * (c % 4):P * (c % 4) + P], vK[:, c, :], ident)
            for c in range(KD):
                x = tr(ps[0:NS, 2 + c // 4, P * (c % 4):P * (c % 4) + P], vN[:, c, :], ident)
            x.then_inc(S["vo_tr"], 1)
            spread(1, 1, mod(1, 2), 4).then_inc(L["gate_mm"], 1)
            pe.wait_ge(S["vo_ok"], 4)
            out_proj(1, zT, (0, 1), (in1[0], in1[1]))
            meet(pe, 11)
            ffn(1, 12)

        @block.scalar
        def _(act):
            fn = nc.scalar.activation

            def copy(out, src, **k):
                return fn(out, src, ACT.Copy, **k)

            def ld(dst, src):
                act.dma_start(dst, src).then_inc(S["params_in"], 16)

            for n in ("xa_ok", "silu_ok", "ht_ok", "ya_ok"):
                act.sem_inc(M[n], AHEAD)
            ld(W[0:1, W_C:W_C + D], a["c_prompt"])
            ld(W[1:9, W_C:W_C + D], a["c_sample"])
            ld(C[:, :], a["consts"])
            ld(W[0:96, 0:P], a["b_ada"].rearrange("l (m p) -> (l m) p", p=P))
            at = 0
            for v in (a["norm_mix_g"].rearrange("l (c p) -> (l c) p", p=P), a["norm_ffn_g"].rearrange("l (c p) -> (l c) p", p=P),
                      a["convb_b"].rearrange("l (c p) -> (l c) p", p=P), a["convb_ln_g"].rearrange("l (c p) -> (l c) p", p=P),
                      a["convb_ln_b"].rearrange("l (c p) -> (l c) p", p=P), a["subln_g"],
                      a["convc_w"].rearrange("l w o (c p) -> (l w o c) p", p=P)):
                ld(W[at:at + v.shape[0], P:2 * P], v)
                at += v.shape[0]
            ld(W[0:124, 2 * P:3 * P], a["convb_w"].rearrange("l w o (c p) -> (l w o c) p", p=P))
            act.dma_start(X[:, 0:4, :], a["x_prompt"][0].rearrange("(i p) d -> p i d", p=P)).then_inc(S["x_in"], 16)
            act.dma_start(X[0:NS, LS, :], a["x_sample"].rearrange("s t d -> (s t) d")).then_inc(S["x_in"], 16)
            act.dma_start(pgt[:, :], a["page_table"].rearrange("s g -> (s g)").rearrange("(o n) -> o n", o=1)).then_inc(
                S["page_in"], 16)
            for q, n in enumerate(("q_norm_g", "k_norm_g")):
                ld(qkg[:, q, :], a[n].rearrange("l m d -> l (m d)").to_broadcast([P, P]))
            for q, n in enumerate(("lam_q1", "lam_k1", "lam_q2", "lam_k2")):
                ld(w(W_LAM, 4, HD)[:, q, :], a[n].to_broadcast([P, HD]))
            for l in range(2):
                ld(rb[:, l, 0:G], a["b_group"][l:l + 1, :].to_broadcast([P, G]))
                ld(rb[:, l, G:NR], a["b_router"][l:l + 1, :].to_broadcast([P, E]))
                ld(wr[:, l, :, 0:G], a["w_group"][l].rearrange("(k p) n -> p k n", p=P))
                ld(wr[:, l, :, G:NR], a["w_router"][l].rearrange("(k p) n -> p k n", p=P))
            act.wait_ge(S["params_in"], 16 * 26)
            fn(W[0:9, W_C:W_C + D], W[0:9, W_C:W_C + D], ACT.Silu).then_inc(S["c_silu"], 1)
            act.wait_ge(S["c_tr"], 1)
            copy(cT[:, :, :].rearrange("p c s -> p (c s)"), ps[:, 7, 0:9 * KD]).then_inc(S["c_ev"], 1)
            act.wait_ge(S["lam_sum"], 1)
            fn(lamw[:, 2:4], lamw[:, 0:2], ACT.Exp).then_inc(S["lam_exp"], 1)

            with act.Fori(0, 4) as it:
                for s in range(NSLOT):
                    n = NSLOT * it + s
                    act.wait_ge(slot_free[s], it + 2)
                    act.wait_ge(S["row_tr"], n + 1)
                    copy(w(W_ROW, 2, 512, rows=9)[:, s % 2, :], ps[0:9, s % 2, :]).then_inc(S["row_ok"], 1)

            def root(out, src, n):
                return fn(out, src, ACT.Sqrt, scale=1.0 / n, bias=epsc[0:src.shape[0], :])

            def rms(l, r):
                for i in range(NT):
                    fn(Hb[0:rows(i), i, :], X[0:rows(i), i, :], ACT.Square,
                       accum_out=st[0:rows(i), i:i + 1]).then_inc(L[f"rms{r}_sum"], 1)
                layer_wait(act, l, f"rms{r}_sum", NT)
                root(st[:, 8:8 + NT], st[:, 0:NT], D).then_inc(L[f"rms{r}_root"], 1)

            def norm(l):
                rms(l, 1)
                layer_wait(act, l, "rms1_inv", 1)
                for i in range(2):
                    fn(Hb[:, i, :], X[:, i, :], ACT.Copy, scale=st[:, 16 + i:17 + i]).then_inc(L["xn_a"], 1)

            def norm_ev(l):
                for c in range(0, KD, 2):
                    layer_wait(act, l, "tr1", c + 1)
                    fn(hT[:, c, 0:TP], ps[:, c % 4, :], ACT.Identity, scale=scT[:, l, c, 0:1],
                       bias=mod(l, 0)[:, c, 0:1]).then_inc(L["ev1a"], 1)

            def gates(l, name):
                layer_wait(act, l, name + "_mm", 1)
                for z in range(2):
                    copy(w(W_G + 512 * z, 512), ps[:, 4 + z, :]).then_inc(L[name + "_ev"], 1)
                    copy(w(W_GS + 512 * z, 512, rows=NS), ps[0:NS, 6 + z, :]).then_inc(L[name + "_ev"], 1)

            act.wait_ge(S["x_in"], 32)
            act.wait_ge(S["stats_set"], 1)
            norm(0)
            meet(act, 0)
            for r in range(2):
                act.dma_start(w(W_CV + 512 * r, 512, rows=120),
                              a["state_conv_b"][0, 4 * r:4 * r + 4].rearrange("s t c -> (s t) c")).then_inc(S["u_state"], 16)
            norm_ev(0)
            for m in range(4):
                act.wait_ge(S["u_mm"], m + 1)
                if m >= 1:
                    act.wait_ge(S["u_ok"], 2 * m)
                fn(sg[:, 0:TP], ps[:, 2 * (m % 2) + 1, :], ACT.Sigmoid).then_inc(S["u_sig"], 1)
                fn(sg[:, TP:T], ps[:, 4 + m % 2, NS:2 * NS], ACT.Sigmoid).then_inc(S["u_sig"], 1)

            def tok_ev(v):
                i, r = v % NT, rows(v % NT)
                act.wait_ge(S["tok_tr"], v + 1)
                fn((QT if v < NT else KT)[:, :, toks(i)], bank(6 + v % 2, H, P)[:, :, 0:r], ACT.Copy,
                   scale=HD ** -0.5 if v < NT else 1.0).then_inc(S["tok_ev"], 1)

            for u in range(3 * NT):
                i, r = u % NT, rows(u % NT)
                act.wait_ge(S["tok_mm"], u + 1)
                if u >= 2 * NT:
                    copy(V[0:r, i, :], ps[0:r, u % 4, :]).then_inc(S["tok_copy"], 1)
                    if u == 2 * NT:
                        tok_ev(u - 1)
                    continue
                if u >= 3:
                    act.wait_ge(S["tok_tr"], u - 2)
                if u - 3 >= NT:
                    act.wait_ge(S["kv_out"], 16 * (u - 3 - NT + 1))
                copy(raw[0:r, u % 3, :], ps[0:r, u % 4, :]).then_inc(S["tok_copy"], 1)
                act.wait_ge(S["tok_copy"], u + 1)
                if u >= 1:
                    act.wait_ge(S["tok_ss"], u)
                fn(sq[0:r, :], raw[0:r, u % 3, :], ACT.Square).then_inc(S["tok_sq"], 1)
                act.wait_ge(S["tok_ss"], u + 1)
                root(st[0:r, 32:40], st[0:r, 24:32], HD).then_inc(S["tok_root"], 1)
                if u >= 1:
                    tok_ev(u - 1)
            meet(act, 1)
            act.wait_ge(S["uo_tr"], 1)
            so = hT[:, :, :].rearrange("p c t -> p (c t)")
            copy(so[0:PAD, 0:512], ps[0:PAD, 6, :]).then_inc(S["uo_ev"], 1)
            copy(so[0:NS, 512:1024], ps[0:NS, 7, :]).then_inc(S["uo_ev"], 1)
            for c in range(4):
                act.wait_ge(S["ln_x"], 2 * c + 2)
                if c >= 2:
                    act.wait_ge(S["ln_mm"], c)
                fn(w(W_RAW, 2, T)[:, c % 2, :], cv[:, c, :], ACT.Square).then_inc(S["ln_sq"], 1)
            act.wait_ge(S["ln_mm"], 5)
            root(sg[:, 0:TP], ps[:, 2, :], 512).then_inc(S["ln_root"], 1)
            root(sg[:, TP:T], ps[:, 3, 0:NS], 512).then_inc(S["ln_root"], 1)
            for c in range(4):
                act.wait_ge(S["ln_n"], c + 1)
                fn(hT[:, 4 + c, :], cv[:, c, :], ACT.Silu, scale=lng[:, c:c + 1], bias=lnb[:, c:c + 1])
            act.wait_ge(S["uo_ev"], 2)
            act.dma_start(o["conv_b_prompt"][0, 0], so[0:PAD, 0:512]).then_inc(S["out_dma"], 16)
            act.dma_start(o["conv_b_sample"][0, :, 0:PAD - TS, :], a["state_conv_b"][0, :, TS:PAD, :]).then_inc(
                S["out_dma"], 16)
            for s in range(NSEQ):
                act.dma_start(o["conv_b_sample"][0, s, PAD - TS:PAD, :], so[TS * s:TS * s + TS, 512:1024]).then_inc(
                    S["out_dma"], 16)
            act.wait_ge(S["out_dma"], 160)
            meet(act, 2)
            act.dma_start(w(0, H * TP), a["prompt_bias"]).then_inc(S["bias_in"], 16)
            e = w(W_E, 4, TP)

            def exps(u):
                n = P * (u % 4 + 1)
                act.wait_ge(S["at_m"], u + 1)
                for m in range(2):
                    fn(e[:, 2 * (u % 2) + m, 0:n], e[:, 2 * (u % 2) + m, 0:n], ACT.Exp, bias=st[:, 4 * (u % 2) + 2 + m:4 * (u % 2) + 3 + m],
                       accum_out=st[:, 8 + 2 * (u % 2) + m:9 + 2 * (u % 2) + m]).then_inc(S["at_e"], 1)

            exps(0)
            for u in range(4 * H):
                h, i = divmod(u, 4)
                if u + 1 < 4 * H:
                    exps(u + 1)
                act.wait_ge(S["at_tr"], u + 1)
                if i == 0 and h >= 1:
                    act.wait_ge(S["at_o"], h)
                copy(w(W_PT, 4, TP)[:, 0:i + 1, P * i:P * i + P], bank(4 + u % 2, i + 1, P)).then_inc(S["at_pt"], 1)
                if i == 3:
                    act.wait_ge(S["at_o"], h + 1)
                    copy(hT[:, h, 0:TP], ps[:, 6 + h % 2, :]).then_inc(S["at_ov"], 1)
            meet(act, 3)
            act.dma_start(w(0, PAST + NSEQ * NS, rows=32), a["sample_bias"]).then_inc(S["bias_in"], 16)
            with act.Fori(0, 4) as it:
                for b in range(2):
                    n = 2 * it + b
                    for q in range(0, 2 * H, 2):
                        act.wait_ge(S["sp_kt"], 8 * n + (q + 1))
                        act.wait_ge(S["sp_s"], 8 * n + max(q, 1))
                        copy(w(W_KT, 2, 512)[:, 0, :], ps[:, 3, :]).then_inc(S["sp_eva"], 1)
                    act.wait_ge(S["sp_d"], 8 * n + 14)
                    fn(w(W_S, PAST + NS, rows=32), w(W_S, PAST + NS, rows=32), ACT.Exp, bias=st[0:32, 5:6],
                       accum_out=st[0:32, 6:7]).then_inc(S["sp_e"], 1)
                    act.wait_ge(S["sp_pt"], n + 2)
                    copy(w(W_PS, 16 * NPG), ps[:, 5, 0:16 * NPG]).then_inc(S["sp_ptev"], 1)
                    copy(w(W_PS + 16 * NPG, 16, rows=NS), ps[0:NS, 5, 16 * NPG:16 * NPG + 16]).then_inc(S["sp_ptev"], 1)
            meet(act, 4)
            for h in range(H):
                if h >= 2:
                    act.wait_ge(S["on_mm"], h - 1)
                fn(w(W_SQ, 2, T)[:, h % 2, :], hT[:, h, :], ACT.Square).then_inc(S["on_sq"], 1)
            act.wait_ge(S["on_mm"], H)
            rn = w(W_RN, H, T)
            for h in range(H):
                root(rn[:, h, 0:TP], ps[:, h, :], 2 * HD).then_inc(S["on_root"], 1)
            root(rn[:, :, TP:T], bank(4, H, NS), 2 * HD).then_inc(S["on_root"], 1)
            meet(act, 5)
            gates(0, "gate")
            meet(act, 6)

            def ffn(l, k0):
                act.dma_start(w(W_SLOT, NB * CAP), a["slot_numbers"]).then_inc(L["slots_in"], 16)
                rms(l, 2)
                layer_wait(act, l, "bc_mm", 1)
                for n, at in enumerate((W_AP, W_AS, W_BP, W_BS)):
                    r = NS if n % 2 else P
                    for z in range(2):
                        copy(w(at + 512 * z, 512, rows=r), ps[0:r, 2 * n + z, :]).then_inc(L["bc_ev"], 1)
                for i in range(NT):
                    layer_wait(act, l, "h_ok", i + 1)
                    act.dma_start(h_dram[toks(i), :], Hb[0:rows(i), i, :]).then_inc(L["h_out"], 16)
                for c in range(0, KD, 2):
                    layer_wait(act, l, "tr2", c + 1)
                    copy(hT[:, c, 0:TP], ps[:, c % 4, :]).then_inc(L["ev2a"], 1)
                layer_wait(act, l, "r_dif", 1)
                fn(st[:, 56:76], st[:, 56:76], ACT.Exp)
                fn(st[:, 76:81], st[:, 76:81], ACT.Exp).then_inc(L["r_exp"], 1)
                layer_wait(act, l, "h_out", 16 * NT)
                meet(act, k0)

                def flat(x):
                    return x.rearrange("p a b -> p (a b)")

                def scaled(j, signal):
                    fn(lane("y", j)[:, 0:512], ps[:, 5, :], ACT.Copy, scale=wj[j][:, :]).then_inc(signal, 1)

                def rows_turned(n, j):
                    act.wait_ge(M["xt_mm"], done(l, n))
                    copy(flat(lane("xt", j)[:, 0:4, :]), ps[:, 0, :]).then_inc(M["xa_ok"], 1)

                def product_out(n, j, p):
                    act.wait_ge(M["down_mm"], done(l, n))
                    act.wait_ge(listed[j], lane_done(l, p, 2))
                    lane_wait(act, scattered, j, l, p - 1, 16)
                    scaled(j, M["ya_ok"])

                def step(n, j, p, first=False, last=False):
                    act.wait_ge(M["gu_mm"], done(l, n))
                    fn(lane("hh", j), ps[:, 2, :], ACT.Silu).then_inc(M["silu_ok"], 1)
                    if not last:
                        rows_turned(n + 1, 1 - j)

                    def one_pass(c, b):
                        act.wait_ge(F["products"], c * 4 - 3)
                        copy(flat(lane("xt", 2)[:, 0:4, :]), ps[:, 0, :]).then_inc(F["act"], 1)
                        act.wait_ge(F["products"], c * 4 - 2)
                        fn(lane("hh", 2), ps[:, 2, :], ACT.Silu).then_inc(F["act"], 1)
                        act.wait_ge(F["products"], c * 4 - 1)
                        copy(flat(lane("ht", 2)), ps[:, 4, :]).then_inc(F["act"], 1)
                        act.wait_ge(F["products"], c * 4)
                        scaled(2, F["act"])

                    further(act, l, n, one_pass)
                    if not first:
                        product_out(n - 1, 1 - j, p - 1 + j)
                    act.wait_ge(M["ht_mm"], done(l, n))
                    copy(flat(lane("ht", j)), ps[:, 4, :]).then_inc(M["ht_ok"], 1)

                rows_turned(0, 0)
                each_expert(act, l, step)
                product_out(E - 1, 1, PAIRS - 1)
                meet(act, k0 + 1)
                yv = y_dram.rearrange("(t k) d -> t (k d)", k=2)
                for i in range(2):
                    act.dma_start(w(W_YB, 2, 2 * D, rows=rows(i))[:, i % 2, :], yv[toks(i), :]).then_inc(L[f"y_in{i % 2}"], 16)
                gates(l, "gate2")
                for i in range(2, NT):
                    layer_wait(act, l, "y_add", i - 1)
                    act.dma_start(w(W_YB, 2, 2 * D, rows=rows(i))[:, i % 2, :], yv[toks(i), :]).then_inc(L[f"y_in{i % 2}"], 16)

            ffn(0, 7)
            meet(act, 9)
            act.dma_start(w(W_ST, D, rows=16), a["state_conv_c"][0].rearrange("s t c -> (s t) c")).then_inc(S["vs_in"], 16)
            norm(1)
            norm_ev(1)
            for c in range(KD):
                act.wait_ge(S["bch_mm"], c + 1)
                if c >= 2:
                    act.wait_ge(S["z_ok"], c - 1)
                g = w(W_CG, 2, T)[:, c % 2, :]
                copy(g[:, 0:TP], ps[:, 4 * (c % 2) + 1, :]).then_inc(S["cg_ok"], 1)
                copy(g[:, TP:T], ps[:, 4 * (c % 2) + 3, NS:2 * NS]).then_inc(S["cg_ok"], 1)
            meet(act, 10)
            act.wait_ge(S["vo_tr"], 1)
            for z in range(2):
                copy(w(W_SO + 512 * z, 512, rows=2), ps[0:2, z, :]).then_inc(S["vo_ok"], 1)
                copy(w(W_ST + 512 * z, 512, rows=NS), ps[0:NS, 2 + z, :]).then_inc(S["vo_ok"], 1)
            act.wait_ge(S["vo_ok"], 4)
            act.dma_start(o["conv_c_prompt"][0, 0], w(W_SO, D, rows=2)).then_inc(S["out_dma"], 16)
            for s in range(NSEQ):
                act.dma_start(o["conv_c_sample"][0, s], W[TS * s + 2:TS * s + 4, W_ST:W_ST + D]).then_inc(S["out_dma"], 16)
            gates(1, "gate")
            act.wait_ge(S["out_dma"], 160 + 144)
            meet(act, 11)
            ffn(1, 12)
            for i in range(NT):
                layer_wait(act, 1, "y_add", i + 1)
                dst = o["y_prompt"][0, toks(i), :] if i < LS else o["y_sample"].rearrange("s t d -> (s t) d")
                act.dma_start(dst, X[0:rows(i), i, :]).then_inc(S["out_dma"], 16)
            act.wait_ge(S["out_dma"], 304 + 16 * NT)

        @block.vector
        def _(dve):
            v = nc.vector
            link = linker(dve, "dve")
            tt, ts, stt = v.tensor_tensor, v.tensor_scalar, v.scalar_tensor_tensor

            def b3(x, n):
                return x.unsqueeze(len(x.shape)).to_broadcast(list(x.shape) + [n])

            for n in ("xd_ok", "h_ok", "yd_ok"):
                dve.sem_inc(M[n], AHEAD)
            v.memset(st[:, :], 1.0).then_inc(S["stats_set"], 1)
            dve.wait_ge(S["params_in"], 16 * 26)
            lv = w(W_LAM, 4, HD)
            for q in range(2):
                link(tt(lv[:, 2 * q, :], lv[:, 2 * q, :], lv[:, 2 * q + 1, :], ALU.mult))
                link(v.tensor_reduce(lamw[:, q:q + 1], lv[:, 2 * q, :], AX, ALU.add))
            link(v.tensor_copy(lamw[:, 5:6], lamw[:, 1:2]))
            v.tensor_copy(lamw[:, 6:7], lamw[:, 0:1]).then_inc(S["lam_sum"], 1)
            dve.wait_ge(S["lam_exp"], 1)
            link(stt(out=neglam, in0=lamw[:, 3:4], scalar=-LAM_INIT, in1=lamw[:, 2:3], op0=ALU.add, op1=ALU.subtract))
            link(stt(out=cmb[:, 0:16], in0=C[0:32, C_SEL + 16:C_SEL + 32], scalar=lamw[0:32, 4:5],
                     in1=C[0:32, C_SEL:C_SEL + 16], op0=ALU.mult, op1=ALU.add))
            dve.wait_ge(S["prm_tr"], 1)
            link(v.tensor_copy(prm[:, :], ps[:, 6, 0:289]))
            link(ts(subg, subg, 1.0 - LAM_INIT, None, ALU.mult))

            def norm(l):
                layer_wait(dve, l, "rms1_root", 1)
                v.reciprocal(st[:, 16:16 + NT], st[:, 8:8 + NT]).then_inc(L["rms1_inv"], 1)
                layer_wait(dve, l, "rms1_inv", 1)
                for i in range(2, NT):
                    ts(Hb[0:rows(i), i, :], X[0:rows(i), i, :], st[0:rows(i), 16 + i:17 + i], None,
                       ALU.mult).then_inc(L["xn_d"], 1)

            dve.sem_inc(S["ada_ev"], 2)
            with dve.Fori(0, 4) as it:
                for s in range(NSLOT):
                    dve.wait_ge(S["row_tr"], NSLOT * it + (s + 3))
                    tt(modT[:, bass.ds(it * 24 + 4 * s, 4), :], bank(2 + s % 2, 4, 9),
                       b3(bT[:, bass.ds(it * 24 + 4 * s, 4)], 9), ALU.add).then_inc(S["ada_ev"], 1)
            dve.wait_ge(S["ada_ev"], 4 * NSLOT + 2)
            norm(0)
            for n in range(4):
                link(stt(out=scT[:, n, :, :], in0=mod(n % 2, 1 if n < 2 else 4), scalar=1.0, in1=b3(gT[:, n, :], 9),
                         op0=ALU.add, op1=ALU.mult))
            meet(dve, 0)

            def norm_ev(l):
                for c in range(1, KD, 2):
                    layer_wait(dve, l, "tr1", c + 1)
                    ts(hT[:, c, 0:TP], ps[:, c % 4, :], scT[:, l, c, 0:1], mod(l, 0)[:, c, 0:1], ALU.mult,
                       ALU.add).then_inc(L["ev1d"], 1)
                layer_wait(dve, l, "tr1", KD + 1)
                hs = hT[:, :, TP:T].rearrange("p c (s t) -> p c s t", t=TS)
                link(tt(hs, bank(4, KD, NSEQ, TS), b3(scT[:, l, :, 1:9], TS), ALU.mult))
                tt(hs, hs, b3(mod(l, 0)[:, :, 1:9], TS), ALU.add).then_inc(L["ev1d"], 1)

            link(v.memset(uT[:, :, 0:PAD], 0.0))
            norm_ev(0)
            for m in range(4):
                dve.wait_ge(S["u_sig"], 2 * m + 2)
                tt(uT[:, m, PAD:PAD + TP], ps[:, 2 * (m % 2), :], sg[:, 0:TP], ALU.mult).then_inc(S["u_ok"], 1)
                tt(uS[:, m, :, PAD:PAD + TS], bank(4 + m % 2, NSEQ, TS), sg[:, TP:T].rearrange("p (s t) -> p s t", t=TS),
                   ALU.mult).then_inc(S["u_ok"], 1)
            dve.wait_ge(S["st_tr"], 1)
            for r in range(2):
                v.tensor_copy(uS[:, :, 4 * r:4 * r + 4, 0:PAD], bank(6 + r, 4, 4, PAD)).then_inc(S["st_ev"], 1)
            dve.wait_ge(S["st_ev"], 2)
            dve.wait_ge(S["u_ok"], 8)

            def conv_tap(n):
                k, c = divmod(n, 4)
                if n >= 4:
                    dve.wait_ge(S["conv"], n - 3)
                if k == 0:
                    x = ts(cv[:, c, 0:TP], uT[:, c, 0:TP], cbw[:, 0, c:c + 1], cbb[:, c:c + 1], ALU.mult, ALU.add)
                else:
                    x = stt(out=cv[:, c, 0:TP], in0=uT[:, c, k:k + TP], scalar=cbw[:, k, c:c + 1], in1=cv[:, c, 0:TP],
                            op0=ALU.mult, op1=ALU.add)
                x.then_inc(S["conv"], 1)

            per = -(-4 * BW // (2 * NT))
            for u in range(2 * NT):
                r = rows(u % NT)
                dve.wait_ge(S["tok_sq"], u + 1)
                v.tensor_reduce(st[0:r, 24:32], sq[0:r, :].rearrange("p (g d) -> p g d", d=HD), AX, ALU.add).then_inc(
                    S["tok_ss"], 1)
                dve.wait_ge(S["tok_root"], u + 1)
                link(v.reciprocal(st[0:r, 40:48], st[0:r, 32:40]))
                rv = raw[0:r, u % 3, :].rearrange("p (g d) -> p g d", d=HD)
                tt(rv, rv, b3(st[0:r, 40:48], HD), ALU.mult).then_inc(S["tok_n"], 1)
                for n in range(per * u, min(per * u + per, 4 * BW)):
                    conv_tap(n)
            for c in range(4):
                for t in range(TS):
                    tmp = sg[:, 0:NSEQ * BW].rearrange("p (s k) -> p s k", k=BW)
                    link(tt(tmp, uS[:, c, :, t:t + BW], cbw[:, :, c].unsqueeze(1).to_broadcast([P, NSEQ, BW]), ALU.mult))
                    link(v.tensor_reduce(cv[:, c, TP + t:T:TS], tmp, AX, ALU.add))
                link(ts(cv[:, c, TP:T], cv[:, c, TP:T], cbb[:, c:c + 1], None, ALU.add))
            meet(dve, 1)
            v.tensor_copy(w(W_SG, 4, NSEQ, TS), uS[:, :, :, PAD:PAD + TS]).then_inc(S["un_ok"], 1)
            dve.wait_ge(S["ln_mm"], 1)
            for c in range(4):
                stt(out=cv[:, c, 0:TP], in0=ps[:, 0, :], scalar=-1.0 / 512, in1=cv[:, c, 0:TP], op0=ALU.mult,
                    op1=ALU.add).then_inc(S["ln_x"], 1)
                stt(out=cv[:, c, TP:T], in0=ps[:, 1, 0:NS], scalar=-1.0 / 512, in1=cv[:, c, TP:T], op0=ALU.mult,
                    op1=ALU.add).then_inc(S["ln_x"], 1)
            dve.wait_ge(S["ln_root"], 2)
            link(v.reciprocal(sg, sg))
            for c in range(4):
                tt(cv[:, c, :], cv[:, c, :], sg, ALU.mult).then_inc(S["ln_n"], 1)
            meet(dve, 2)
            dve.wait_ge(S["bias_in"], 16)
            e = w(W_E, 4, TP)
            bias = w(0, H, TP)

            def maxima(u):
                h, i = divmod(u, 4)
                n, s = P * (i + 1), 4 * (u % 2)
                dve.wait_ge(S["at_s"], u + 1)
                if u >= 2:
                    dve.wait_ge(S["at_tr"], u - 1)
                for m in range(2):
                    v.tensor_tensor_reduce(out=e[:, 2 * (u % 2) + m, 0:n], in0=ps[:, 2 * (u % 2) + m, 0:n],
                                           in1=bias[:, h, TP - n:TP], scale=1.0, scalar=-3e38, op0=ALU.add, op1=ALU.max,
                                           accum_out=st[:, s + m:s + m + 1]).then_inc(S["at_b"], 1)
                dve.wait_ge(S["at_b"], 2 * u + 2)
                ts(st[:, s + 2:s + 4], st[:, s:s + 2], -1.0, None, ALU.mult).then_inc(S["at_m"], 1)

            maxima(0)
            for u in range(4 * H):
                n = P * (u % 4 + 1)
                if u + 1 < 4 * H:
                    maxima(u + 1)
                dve.wait_ge(S["at_e"], 2 * u + 2)
                at = 12 + 2 * (u % 2)
                link(v.reciprocal(st[:, at:at + 2], st[:, 8 + 2 * (u % 2):10 + 2 * (u % 2)]))
                link(ts(st[:, 16:17], st[:, at + 1:at + 2], neglam, None, ALU.mult))
                e0, e1 = e[:, 2 * (u % 2), 0:n], e[:, 2 * (u % 2) + 1, 0:n]
                link(ts(e1, e1, st[:, 16:17], None, ALU.mult))
                stt(out=e0, in0=e0, scalar=st[:, at:at + 1], in1=e1, op0=ALU.mult, op1=ALU.add).then_inc(S["at_p"], 1)
            meet(dve, 3)
            qb = w(W_QB, NSEQ, H, 32)
            link(v.memset(qb, 0.0))
            for h in range(H):
                for m in range(2):
                    link(v.tensor_copy(qb[HD * m:HD * m + HD, :, h, 8 * h + 4 * m:8 * h + 4 * m + 4],
                                       QT[HD * m:HD * m + HD, h, TP:T].rearrange("p (s t) -> p s t", t=TS)))
            dve.sem_inc(S["sp_d"], 8)
            dve.sem_inc(S["sp_ov"], 1)
            dve.wait_ge(S["bias_in"], 32)
            sb_ = w(W_S, PAST + NS, rows=32)
            bs = w(0, PAST + NSEQ * NS, rows=32)
            with dve.Fori(0, 4) as it:
                for b in range(2):
                    n = 2 * it + b
                    dve.wait_ge(slot_free[2 - 2 * b], it + (5 + b))
                    v.tensor_copy(w(W_QC, 4 * 32), qb.rearrange("p s h c -> p s (h c)")[:, bass.ds(n, 1), :].rearrange(
                        "p o c -> p (o c)")).then_inc(S["sp_q"], 1)
                    for q in range(1, 2 * H, 2):
                        dve.wait_ge(S["sp_kt"], 8 * n + (q + 1))
                        dve.wait_ge(S["sp_s"], 8 * n + q)
                        v.tensor_copy(w(W_KT, 2, 512)[:, 1, :], ps[:, 4, :]).then_inc(S["sp_evd"], 1)
                    dve.wait_ge(slot_free[2 * b], it + 6)
                    dve.wait_ge(S["sp_pt"], n + 1)
                    carry(dve)
                    for half in range(2):
                        v.tensor_tensor_reduce(out=sb_[:, 512 * half:512 * half + 512], in0=ps[0:32, half, :],
                                               in1=bs[:, 512 * half:512 * half + 512], scale=1.0, scalar=-3e38,
                                               op0=ALU.add, op1=ALU.max, accum_out=st[0:32, half:half + 1]).then_inc(S["sp_d"], 1)
                    tt(sb_[:, PAST:PAST + NS], ps[0:32, 2, 0:NS], bs[:, bass.ds(n * NS + PAST, NS)], ALU.add).then_inc(
                        S["sp_d"], 1)
                    dve.wait_ge(S["sp_d"], 8 * n + 11)
                    v.tensor_reduce(st[0:32, 2:3], sb_[:, PAST:PAST + NS], AX, ALU.max).then_inc(S["sp_d"], 1)
                    dve.wait_ge(S["sp_d"], 8 * n + 12)
                    v.tensor_reduce(st[0:32, 4:5], st[0:32, 0:3], AX, ALU.max).then_inc(S["sp_d"], 1)
                    dve.wait_ge(S["sp_d"], 8 * n + 13)
                    ts(st[0:32, 5:6], st[0:32, 4:5], -1.0, None, ALU.mult).then_inc(S["sp_d"], 1)
                    dve.wait_ge(S["sp_e"], n + 1)
                    v.reciprocal(st[0:32, 7:8], st[0:32, 6:7]).then_inc(S["sp_d"], 1)
                    dve.wait_ge(S["sp_d"], 8 * n + 15)
                    ts(cmb[:, 16:32], cmb[:, 0:16], st[0:32, 7:8], None, ALU.mult).then_inc(S["sp_d"], 1)
                    dve.wait_ge(slot_free[2 * b + 1], it + 6)
                    v.tensor_copy(hT[:, 0:H, bass.ds(n * TS + TP, TS)], bank(6, H, TS)).then_inc(S["sp_ov"], 1)
            meet(dve, 4)
            dve.wait_ge(S["on_root"], H + 1)
            rn = w(W_RN, H, T)
            link(v.reciprocal(rn, rn))
            for h in range(H):
                stt(out=hT[:, h, :], in0=hT[:, h, :], scalar=subg, in1=rn[:, h, :], op0=ALU.mult,
                    op1=ALU.mult).then_inc(S["on_ok"], 1)
            meet(dve, 5)

            def repeat(src, at=W_RA):
                v.tensor_copy(w(at, KD, NSEQ, TS), b3(src[:, :, 1:9], TS)).then_inc(L["rep_ok"], 1)

            def out_mul(l):
                repeat(mod(l, 2))
                layer_wait(dve, l, "gate_ev", 4)
                for u in range(2 * NT):
                    z, i = divmod(u, NT)
                    layer_wait(dve, l, "wo_mm", u + 1)
                    if u >= 2:
                        layer_wait(dve, l, "wo_add", u - 1)
                    tt(w(W_YB, 2, 512, rows=rows(i))[:, u % 2, :], ps[0:rows(i), u % 4, :],
                       w((W_G if i < LS else W_GS) + 512 * z, 512, rows=rows(i)), ALU.mult).then_inc(L["wo_mul"], 1)

            out_mul(0)
            meet(dve, 6)

            def ffn(l, k0):
                repeat(scT[:, 2 + l, :, :])
                repeat(mod(l, 3), W_RB)
                layer_wait(dve, l, "rms2_root", 1)
                link(v.reciprocal(st[:, 16:16 + NT], st[:, 8:8 + NT]))
                layer_wait(dve, l, "bc_ev", 8)
                for i in range(NT):
                    stt(out=Hb[0:rows(i), i, :], in0=X[0:rows(i), i, :], scalar=st[0:rows(i), 16 + i:17 + i],
                        in1=w(W_AP if i < LS else W_AS, D, rows=rows(i)), op0=ALU.mult, op1=ALU.mult).then_inc(
                        L["h_mul"], 1)
                for c in range(1, KD, 2):
                    layer_wait(dve, l, "tr2", c + 1)
                    v.tensor_copy(hT[:, c, 0:TP], ps[:, c % 4, :]).then_inc(L["ev2d"], 1)
                layer_wait(dve, l, "tr2", KD + 1)
                v.tensor_copy(hT[:, :, TP:T], bank(4, KD, NS)).then_inc(L["ev2d"], 1)

                lg = w(R_LG, NT, NR)
                me, a1, a2, cc, t1, m2 = (w(x, NT, E) for x in (R_ME, R_A1, R_A2, R_CC, R_T, R_M2))
                i32, i32m, grpm = (C[:, x:x + E].unsqueeze(1).to_broadcast([P, NT, E]) for x in (C_I32, C_I32M, C_GRPM))
                valid = C[:, C_VALID:C_VALID + NT]
                link(v.memset(lg, 0.0))
                layer_wait(dve, l, "lg_mm", 1)
                link(tt(lg[:, 0:LS, :], bank(5, LS, NR), rb[:, l:l + 1, :].to_broadcast([P, LS, NR]), ALU.add))
                link(tt(lg[0:NS, LS, :], ps[0:NS, 5, NR * LS:NR * NT], rb[0:NS, l, :], ALU.add))
                gm, gi, v1, v2, i1 = (st[:, x:x + NT] for x in (24, 29, 34, 39, 44))
                tg = t1[:, :, 0:G]
                link(v.tensor_reduce(gm, lg[:, :, 0:G], AX, ALU.max))
                link(tt(tg, lg[:, :, 0:G], b3(gm, G), ALU.is_equal))
                link(stt(out=tg, in0=tg, scalar=-99.0, in1=C[:, C_I32:C_I32 + G].unsqueeze(1).to_broadcast([P, NT, G]),
                         op0=ALU.mult, op1=ALU.add))
                link(v.tensor_reduce(gi, tg, AX, ALU.min))
                link(tt(t1, grpm, b3(gi, E), ALU.is_equal))
                link(ts(t1, t1, -1.0, BIG, ALU.add, ALU.mult))
                link(tt(me, lg[:, :, G:NR], t1, ALU.add))
                for src, top, hot in ((me, v1, a1), (m2, v2, a2)):
                    link(v.tensor_reduce(top, src, AX, ALU.max))
                    link(tt(t1, src, b3(top, E), ALU.is_equal))
                    link(stt(out=t1, in0=t1, scalar=-99.0, in1=i32, op0=ALU.mult, op1=ALU.add))
                    link(v.tensor_reduce(i1, t1, AX, ALU.min))
                    link(tt(hot, i32m, b3(i1, E), ALU.is_equal))
                    if src is me:
                        link(stt(out=m2, in0=hot, scalar=-3e38, in1=me, op0=ALU.mult, op1=ALU.add))
                for hot in (a1, a2):
                    link(tt(hot, hot, b3(valid, E), ALU.mult))
                link(tt(cc, a1, a2, ALU.add))
                link(tt(st[:, 56:76].rearrange("p (i g) -> p i g", g=G), lg[:, :, 0:G], b3(gm, G), ALU.subtract))
                link(tt(st[:, 76:81], v2, v1, ALU.subtract))
                v.tensor_copy(st[:, 86:87], st[:, 80:81]).then_inc(L["r_dif"], 1)
                v.tensor_copy(st[:, 87:88], st[:, 24:25]).then_inc(L["r_ok"], 1)
                layer_wait(dve, l, "r_exp", 1)
                gs, w1, w2 = st[:, 81:86], st[:, 49:54], st[:, 88:93]
                link(v.tensor_reduce(gs, st[:, 56:76].rearrange("p (i g) -> p i g", g=G), AX, ALU.add))
                link(stt(out=w1, in0=st[:, 76:81], scalar=1.0, in1=gs, op0=ALU.add, op1=ALU.mult))
                link(v.reciprocal(w1, w1))
                link(tt(w2, w1, st[:, 76:81], ALU.mult))
                v3 = w(W_V3, NT, 2, 3, E)
                for q, (hot, wk) in enumerate(((a1, w1), (a2, w2))):
                    a1c = C[:, C_A1:C_A1 + 2 * NT].rearrange("p (i k) -> p i k", k=2)[:, :, q]
                    for z, val in enumerate((a1c, C[:, C_T:C_T + NT], wk)):
                        link(tt(v3[:, :, q, z, :], hot, b3(val, E), ALU.mult))
                layer_wait(dve, l, "cnt_mm", 1)
                for q, hot in enumerate((a1, a2)):
                    link(tt(t1, hot, bank(6, NT, E), ALU.mult))
                    link(v.tensor_reduce(st[:, 24 + NT * q:24 + NT * q + NT], t1, AX, ALU.add))
                cnt, nbp = w(R_ME, E, rows=1), w(R_M2, E, rows=1)
                link(v.tensor_copy(cnt, ps[0:1, 6, E * NT:E * NT + E]))
                link(v.memset(nbp, 1.0))
                for b in range(1, NB):
                    link(stt(out=nbp, in0=cnt, scalar=float(CAP * b), in1=nbp, op0=ALU.is_gt, op1=ALU.add))
                if l == 0:
                    link(v.memset(tabf[:, :, :], 0.0))
                extra, inc, tmp = tabf[:, 0, 0:E], tabf[:, 1, 0:E], tabf[:, 2, 0:E]
                link(ts(extra, nbp, -1.0, None, ALU.add))
                link(v.tensor_copy(inc, extra))
                for b in (1, 2, 4, 8, 16):
                    link(v.tensor_copy(tmp, inc))
                    link(tt(inc[:, b:E], tmp[:, b:E], tmp[:, 0:E - b], ALU.add))
                link(stt(out=tmp, in0=inc, scalar=tabf[:, 3, 0:1], in1=extra, op0=ALU.add, op1=ALU.subtract))
                link(tt(tabf[:, 3, 0:1], tabf[:, 3, 0:1], inc[:, E - 1:E], ALU.add))
                link(v.tensor_copy(tab[l][:, 0, :], nbp))
                v.tensor_copy(tab[l][:, 1, :], tmp).then_inc(L["bounds"], 1)
                layer_wait(dve, l, "slots_in", 16)
                for q in range(2 * NT):
                    i, k = divmod(q, 2)
                    if q >= 2:
                        layer_wait(dve, l, "list_mm", q - 1)
                    ts(w(W_OH, 2, NB * CAP)[:, q % 2, :], w(W_SLOT, NB * CAP), st[:, 24 + NT * k + i:25 + NT * k + i],
                       None, ALU.is_equal).then_inc(L["oh_ok"], 1)
                layer_wait(dve, l, "list_mm", 2 * NT)
                li = w(W_LI, NB, E, 2, rows=CAP).bitcast(I32)
                lw = w(W_LW, NB, E, rows=CAP)
                for b0, nb in ((0, NB),):
                    pv = bank(0, nb, 3, E, rows=CAP)
                    row = w(W_OH, nb, E, rows=CAP)
                    link(ts(row, pv[:, :, 0, :], 0.0, OOB, ALU.is_equal, ALU.mult))
                    link(stt(out=row, in0=pv[:, :, 0, :], scalar=-1.0, in1=row, op0=ALU.add, op1=ALU.add))
                    link(v.tensor_copy(li[:, b0:b0 + nb, :, 1], row))
                    link(v.tensor_copy(li[:, b0:b0 + nb, :, 0], pv[:, :, 1, :]))
                    link(v.tensor_copy(lw[:, b0:b0 + nb, :], pv[:, :, 2, :]))
                meet(dve, k0)

                def flat(x):
                    return x.rearrange("p a b -> p (a b)")

                def scaled(j, signal):
                    ts(lane("y", j)[:, 512:D], ps[:, 6, :], wj[j][:, :], None, ALU.mult).then_inc(signal, 1)

                def rows_turned(n, j):
                    dve.wait_ge(M["xt_mm"], done(l, n))
                    v.tensor_copy(flat(lane("xt", j)[:, 4:8, :]), ps[:, 1, :]).then_inc(M["xd_ok"], 1)

                def product_out(n, j, p):
                    dve.wait_ge(M["down_mm"], done(l, n))
                    dve.wait_ge(listed[j], lane_done(l, p, 2))
                    lane_wait(dve, scattered, j, l, p - 1, 16)
                    scaled(j, M["yd_ok"])

                def step(n, j, p, first=False, last=False):
                    dve.wait_ge(M["silu_ok"], done(l, n))
                    tt(lane("hh", j), lane("hh", j), ps[:, 3, :], ALU.mult).then_inc(M["h_ok"], 1)
                    if not last:
                        rows_turned(n + 1, 1 - j)

                    def one_pass(c, b):
                        dve.wait_ge(F["products"], c * 4 - 3)
                        v.tensor_copy(flat(lane("xt", 2)[:, 4:8, :]), ps[:, 1, :]).then_inc(F["dve"], 1)
                        dve.wait_ge(F["act"], c * 4 - 2)
                        tt(lane("hh", 2), lane("hh", 2), ps[:, 3, :], ALU.mult).then_inc(F["dve"], 1)
                        dve.wait_ge(F["products"], c * 4)
                        scaled(2, F["dve"])

                    further(dve, l, n, one_pass)
                    if not first:
                        product_out(n - 1, 1 - j, p - 1 + j)

                rows_turned(0, 0)
                each_expert(dve, l, step)
                product_out(E - 1, 1, PAIRS - 1)
                meet(dve, k0 + 1)
                repeat(mod(l, 5))
                layer_wait(dve, l, "gate2_ev", 4)
                for i in range(NT):
                    y = w(W_YB, 2, 2, D, rows=rows(i))[:, i % 2]
                    layer_wait(dve, l, f"y_in{i % 2}", 16 * (i // 2) + 16)
                    link(tt(y[:, 0, :], y[:, 0, :], y[:, 1, :], ALU.add))
                    tt(y[:, 0, :], y[:, 0, :], w(W_G if i < LS else W_GS, D, rows=rows(i)), ALU.mult).then_inc(
                        L["y_mul"], 1)

            ffn(0, 7)
            meet(dve, 9)
            norm(1)
            norm_ev(1)
            vp, y3 = w(W_VP, 2 + TP), w(W_Y3, T)
            link(v.memset(vp[:, 0:2], 0.0))
            dve.wait_ge(S["vs_tr"], 1)
            v.tensor_copy(vS[:, :, :, 0:2], bank(7, KD, NSEQ, 2)).then_inc(S["vs_ok"], 1)
            dve.wait_ge(S["vs_ok"], 1)
            y3s = y3[:, TP:T].rearrange("p (s t) -> p s t", t=TS)
            for c in range(KD):
                b = 4 * (c % 2)
                g = w(W_CG, 2, T)[:, c % 2, :]
                dve.wait_ge(S["cg_ok"], 2 * c + 2)
                link(tt(vp[:, 2:2 + TP], g[:, 0:TP], ps[:, b + 2, :], ALU.mult))
                link(tt(vS[:, c, :, 2:2 + TS], g[:, TP:T].rearrange("p (s t) -> p s t", t=TS),
                        bank(b + 3, NSEQ, TS, at=2 * NS), ALU.mult))
                link(v.tensor_copy(vK[:, c, :], vp[:, TP:TP + 2]))
                link(v.tensor_copy(vN[:, c, :].rearrange("p (s t) -> p s t", t=TS), vS[:, c, :, 2:2 + TS]))
                link(ts(y3[:, 0:TP], vp[:, 0:TP], ccw[:, 0, c:c + 1], None, ALU.mult))
                link(ts(y3s, vS[:, c, :, 0:TS], ccw[:, 0, c:c + 1], None, ALU.mult))
                for k in (1, 2):
                    link(stt(out=y3[:, 0:TP], in0=vp[:, k:k + TP], scalar=ccw[:, k, c:c + 1], in1=y3[:, 0:TP],
                             op0=ALU.mult, op1=ALU.add))
                    link(stt(out=y3s, in0=vS[:, c, :, k:k + TS], scalar=ccw[:, k, c:c + 1], in1=y3s,
                             op0=ALU.mult, op1=ALU.add))
                link(tt(zT[:, c, 0:TP], y3[:, 0:TP], ps[:, b, :], ALU.mult))
                tt(zT[:, c, TP:T], y3[:, TP:T], ps[:, b + 3, 0:NS], ALU.mult).then_inc(S["z_ok"], 1)
            meet(dve, 10)
            out_mul(1)
            meet(dve, 11)
            ffn(1, 12)

        @block.gpsimd
        def _(pool):
            g = nc.gpsimd
            meet(pool, 0)
            for u in range(2 * NT):
                i, r = u % NT, rows(u % NT)
                pool.wait_ge(S["tok_n"], u + 1)
                rv = raw[0:r, u % 3, :].rearrange("p (h d) -> p h d", h=H)
                g.tensor_tensor(rv, rv, qkg[0:r, u // NT:u // NT + 1, :].to_broadcast([r, H, P]), ALU.mult).then_inc(
                    S["tok_g"], 1)
                if u >= NT:
                    pool.wait_ge(S["tok_g"], u + 1)
                    if u > NT:
                        pool.wait_ge(S["kv_out"], 16 * (u - NT))
                    dst = (o["k_prompt"][0, 0, toks(i)].rearrange("t h d -> t (h d)") if i < LS
                           else o["k_sample"][0].rearrange("s t h d -> (s t) (h d)"))
                    pool.dma_start(dst, raw[0:r, u % 3, :]).then_inc(S["kv_out"], 16)
            for i in range(NT):
                pool.wait_ge(S["tok_copy"], 2 * NT + i + 1)
                dst = (o["v_prompt"][0, 0, toks(i)].rearrange("t h d -> t (h d)") if i < LS
                       else o["v_sample"][0].rearrange("s t h d -> (s t) (h d)"))
                pool.dma_start(dst, V[0:rows(i), i, :]).then_inc(S["kv_out"], 16)
            pool.wait_ge(S["kv_out"], 32 * NT)
            for k in range(1, 6):
                meet(pool, k)

            def out_add(l):
                for u in range(2 * NT):
                    z, i = divmod(u, NT)
                    layer_wait(pool, l, "wo_mul", u + 1)
                    xv = X[0:rows(i), i, 512 * z:512 * z + 512]
                    g.tensor_tensor(xv, xv, w(W_YB, 2, 512, rows=rows(i))[:, u % 2, :], ALU.add).then_inc(
                        L["wo_add"], 1)

            out_add(0)
            meet(pool, 6)

            def ffn(l, k0):
                layer_wait(pool, l, "bc_ev", 8)
                for i in range(NT):
                    layer_wait(pool, l, "h_mul", i + 1)
                    hv = Hb[0:rows(i), i, :]
                    g.tensor_tensor(hv, hv, w(W_BP if i < LS else W_BS, D, rows=rows(i)), ALU.add).then_inc(
                        L["h_ok"], 1)
                meet(pool, k0)
                li = w(W_LI, NB * E, 2, rows=CAP).bitcast(I32)
                lw = w(W_LW, NB * E, rows=CAP)

                def gather_rows(j, col, signal):
                    g.tensor_copy(gix[j][:, :], li[:, bass.ds(col, 1), 0]).then_inc(signal[0], 1)
                    pool.wait_ge(*signal[1])
                    carry(pool)
                    g.indirect_dma_start(out=lane("xg", j).rearrange("p a b -> p (a b)"), out_offset=None, in_=h_dram,
                                         in_offset=bass.IndirectOffsetOnAxis(ap=gix[j][:, 0:1], axis=0),
                                         bounds_check=T - 1, oob_is_err=False).then_inc(signal[2], 16)

                def lists(j, col, signal):
                    g.tensor_copy(six[j][:, :], li[:, bass.ds(col, 1), 1]).then_inc(signal, 1)
                    g.tensor_copy(wj[j][:, :], lw[:, bass.ds(col, 1)]).then_inc(signal, 1)

                def scatter_rows(j, signal):
                    carry(pool)
                    g.indirect_dma_start(out=y_dram, out_offset=bass.IndirectOffsetOnAxis(ap=six[j][:, 0:1], axis=0),
                                         in_=lane("y", j), in_offset=None,
                                         bounds_check=2 * T - 1, oob_is_err=False).then_inc(signal, 16)

                def gather(n, j, p):
                    lane_wait(pool, gathered, j, l, p - 1, 16)
                    pool.wait_ge(M["xt_mm"], done(l, n - 2))
                    carry(pool)
                    gather_rows(j, n, (gix_ok[j], (gix_ok[j], lane_done(l, p, 1)), gathered[j]))

                def scatter(n, j, p):
                    pool.wait_ge(M["ya_ok"], done(l, n))
                    pool.wait_ge(M["yd_ok"], done(l, n))
                    pool.wait_ge(listed[j], lane_done(l, p, 2))
                    scatter_rows(j, scattered[j])

                def step(n, j, p, first=False, last=False):
                    if first or (j == 1 and not last):
                        gather(n + 2, j, p + 1)
                    elif not last and isinstance(p, int):
                        gather(n + 2, j, p + 1)
                    elif not last:
                        with pool.If(p < PAIRS - 1):
                            gather(n + 2, j, p + 1)
                        pool.nop()
                    lane_wait(pool, scattered, j, l, p - 1, 16)
                    carry(pool)
                    lists(j, n, listed[j])

                    def one_pass(c, b):
                        lists(2, b * E + n, F["listed"])
                        gather_rows(2, b * E + n, (F["listed"], (F["listed"], c * 3), F["gathered"]))
                        pool.wait_ge(F["act"], c * 4)
                        pool.wait_ge(F["dve"], c * 3)
                        scatter_rows(2, F["scattered"])
                        pool.wait_ge(F["scattered"], c * 16)
                        carry(pool)

                    further(pool, l, n, one_pass)
                    if not first:
                        scatter(n - 1, 1 - j, p - 1 + j)

                gather(0, 0, 0)
                gather(1, 1, 0)
                each_expert(pool, l, step)
                scatter(E - 1, 1, PAIRS - 1)
                for j in range(2):
                    pool.wait_ge(scattered[j], lane_done(l, PAIRS - 1, 16))
                meet(pool, k0 + 1)
                for i in range(NT):
                    layer_wait(pool, l, "y_mul", i + 1)
                    xv = X[0:rows(i), i, :]
                    g.tensor_tensor(xv, xv, w(W_YB, 2, 2, D, rows=rows(i))[:, i % 2, 0, :], ALU.add).then_inc(
                        L["y_add"], 1)

            ffn(0, 7)
            meet(pool, 9)
            meet(pool, 10)
            out_add(1)
            meet(pool, 11)
            ffn(1, 12)


_INS = ["x_prompt", "x_sample", "cache_k", "cache_v", "state_conv_b", "state_conv_c", "page_table", "c_prompt",
        "c_sample", "norm_mix_g", "norm_ffn_g", "w_ada", "b_ada", "w_in_a", "q_norm_g", "k_norm_g", "lam_q1", "lam_k1",
        "lam_q2", "lam_k2", "subln_g", "convb_w", "convb_b", "convb_ln_g", "convb_ln_b", "w_out_a", "w_in_c", "convc_w",
        "w_out_c", "w_group", "b_group", "w_router", "b_router", "w_gate_up", "w_down"]
_OUTS = [("y_prompt", (1, TP, D)), ("y_sample", (NSEQ, TS, D)), ("k_prompt", (1, 1, TP, H, P)),
         ("v_prompt", (1, 1, TP, H, P)), ("k_sample", (1, NSEQ, TS, H, P)), ("v_sample", (1, NSEQ, TS, H, P)),
         ("conv_b_prompt", (1, 1, PAD, 512)), ("conv_b_sample", (1, NSEQ, PAD, 512)),
         ("conv_c_prompt", (1, 1, 2, D)), ("conv_c_sample", (1, NSEQ, 2, D))]


def kernel(**inputs):
    import concourse.bacc as _bacc
    from concourse.bass_utils import run_bass_kernel_spmd as _run

    nc = _bacc.Bacc("TRN2", target_bir_lowering=False, num_devices=1)
    arrays, a = {}, {}
    given = {n: inputs[n] for n in _INS}
    given.update(consts=constants(), prompt_bias=prompt_bias(), sample_bias=sample_bias(), slot_numbers=slot_numbers())
    for name, x in given.items():
        x = np.ascontiguousarray(x)
        arrays[f"in_{name}_dram"] = x
        a[name] = nc.dram_tensor(f"in_{name}_dram", x.shape, mybir.dt.from_np(x.dtype), kind="ExternalInput").ap()
    o = {name: nc.dram_tensor(f"out_{name}_dram", shape, F32, kind="ExternalOutput").ap() for name, shape in _OUTS}
    hybrid_step(nc, a, o)
    r = _run(nc, [arrays], core_ids=[0])
    return tuple(r.results[0][f"out_{name}_dram"] for name, _ in _OUTS)
```
